# Optimizing a Trainium2 kernel written in Bass

```python
import math
import jax, jax.numpy as jnp
from jax import lax
import numpy as np

D_MODEL = 2048
BATCH = 1
SEQ = 256
DEPTH = 2

SB_HEADS = 8
SB_HEAD_DIM = 128
SB_WIDTH = SB_HEADS * SB_HEAD_DIM
QUERY_BLOCK = 128
SSM_WIDTH = D_MODEL // 4
SSM_GROUP = 16
SSM_GROUPS = SSM_WIDTH // SSM_GROUP
SSM_STATE = 64
SCAN_CHUNK = 128
DT_MIN = 1e-3
DT_MAX = 1e-1
MEM_TOKENS = 256
MEM_HEADS = 4
MEM_HEAD_DIM = 128
MEM_WIDTH = MEM_HEADS * MEM_HEAD_DIM
N_BRANCHES = 3
IN_WIDTH = 3 * SB_WIDTH + SSM_WIDTH + MEM_WIDTH + N_BRANCHES * D_MODEL
D_FF = ((8 * D_MODEL + 3 * 256 - 1) // (3 * 256)) * 256
DN_ALPHA = (2 * DEPTH) ** 0.25
DN_BETA = (8 * DEPTH) ** -0.25
LN_EPS = 1e-5

kernel_name = "hybrid_sb_s5_mem_deepnorm"

def _layer_norm(x, g, b):
    xf = x.astype(jnp.float32)
    mu = jnp.mean(xf, axis=-1, keepdims=True)
    var = jnp.mean(jnp.square(xf - mu), axis=-1, keepdims=True)
    return ((xf - mu) * lax.rsqrt(var + LN_EPS) * g + b).astype(x.dtype)

def _stick_breaking_attention(q, k, v):
    bsz, seq, heads, dh = q.shape
    scale = dh ** -0.5
    outs = []
    for i in range(seq // QUERY_BLOCK):
        q0 = i * QUERY_BLOCK
        k_end = q0 + QUERY_BLOCK
        z = jnp.einsum('bqhd,bkhd->bhqk', q[:, q0:k_end], k[:, :k_end]).astype(jnp.float32) * scale
        t_idx = q0 + jnp.arange(QUERY_BLOCK)
        s_idx = jnp.arange(k_end)
        causal = s_idx[None, :] < t_idx[:, None]
        log1m = jnp.where(causal, jax.nn.log_sigmoid(-z), 0.0)
        after = lax.cumsum(log1m, axis=3, reverse=True) - log1m
        logw = jnp.where(causal, jax.nn.log_sigmoid(z) + after, -jnp.inf)
        w = jnp.exp(logw).astype(v.dtype)
        outs.append(jnp.einsum('bhqk,bkhd->bqhd', w, v[:, :k_end]))
    return jnp.concatenate(outs, axis=1)

def _ssm_combine(left, right):
    a1, b1 = left
    a2, b2 = right
    return a1 * a2, a2 * b1 + b2

def _s5(u, lam_re, lam_im, log_dt, b_re, b_im, c_re, c_im, d_skip):
    f32 = jnp.float32
    bsz, seq, _ = u.shape
    uf = u.astype(f32)
    lam = lax.complex(lam_re.astype(f32), lam_im.astype(f32))
    dt = jnp.exp(log_dt.astype(f32))[:, None]
    lam_bar = jnp.exp(lam * dt)
    b_bar = ((lam_bar - 1.0) / lam)[..., None] * lax.complex(b_re.astype(f32), b_im.astype(f32))
    c = lax.complex(c_re.astype(f32), c_im.astype(f32))
    n_chunks = seq // SCAN_CHUNK
    u_chunks = uf.reshape(bsz, n_chunks, SCAN_CHUNK, SSM_GROUPS, SSM_GROUP).transpose(1, 0, 2, 3, 4)

    def chunk_step(h_prev, uc):
        bu = jnp.einsum('gpc,btgc->btgp', b_bar, uc.astype(jnp.complex64))
        a = jnp.broadcast_to(lam_bar, bu.shape)
        a_cum, h_loc = lax.associative_scan(_ssm_combine, (a, bu), axis=1)
        h_all = h_loc + a_cum * h_prev[:, None]
        y = jnp.real(jnp.einsum('gcp,btgp->btgc', c, h_all))
        return h_all[:, -1], y

    h0 = jnp.zeros((bsz, SSM_GROUPS, SSM_STATE), jnp.complex64)
    _, ys = lax.scan(chunk_step, h0, u_chunks)
    y = ys.transpose(1, 0, 2, 3, 4).reshape(bsz, seq, SSM_WIDTH)
    return y + d_skip.astype(f32) * uf

def _memory_attention(q, mem, w_kv):
    bsz, seq, _ = q.shape
    kv = jnp.einsum('bmd,de->bme', mem, w_kv)
    k, v = jnp.split(kv, 2, axis=-1)
    qh = q.reshape(bsz, seq, MEM_HEADS, MEM_HEAD_DIM)
    kh = k.reshape(bsz, MEM_TOKENS, MEM_HEADS, MEM_HEAD_DIM)
    vh = v.reshape(bsz, MEM_TOKENS, MEM_HEADS, MEM_HEAD_DIM)
    s = jnp.einsum('blhd,bmhd->bhlm', qh, kh).astype(jnp.float32) * (MEM_HEAD_DIM ** -0.5)
    p = jax.nn.softmax(s, axis=-1).astype(v.dtype)
    return jnp.einsum('bhlm,bmhd->blhd', p, vh).reshape(bsz, seq, MEM_WIDTH)

def setup_inputs(seed: int = 0) -> dict:
    key = jax.random.key(seed)
    ks = jax.random.split(key, 24)
    f32 = jnp.float32

    def nrm(k, shape, scale):
        return jax.random.normal(k, shape, f32) * scale

    n_idx = jnp.arange(SSM_STATE, dtype=f32)
    lam_im_base = jnp.broadcast_to(math.pi * n_idx, (DEPTH, SSM_GROUPS, SSM_STATE))
    return {
        "x": nrm(ks[0], (BATCH, SEQ, D_MODEL), 1.0),
        "mem": nrm(ks[1], (BATCH, MEM_TOKENS, D_MODEL), 1.0),
        "w_in": nrm(ks[2], (DEPTH, D_MODEL, IN_WIDTH), D_MODEL ** -0.5),
        "b_in": nrm(ks[3], (DEPTH, IN_WIDTH), 0.02),
        "sb_w_out": nrm(ks[4], (DEPTH, SB_WIDTH, D_MODEL), SB_WIDTH ** -0.5),
        "ssm_lambda_re": -0.5 + nrm(ks[5], (DEPTH, SSM_GROUPS, SSM_STATE), 0.01),
        "ssm_lambda_im": lam_im_base + nrm(ks[6], (DEPTH, SSM_GROUPS, SSM_STATE), 0.01),
        "ssm_log_dt": jax.random.uniform(ks[7], (DEPTH, SSM_GROUPS), f32, math.log(DT_MIN), math.log(DT_MAX)),
        "ssm_b_re": nrm(ks[8], (DEPTH, SSM_GROUPS, SSM_STATE, SSM_GROUP), (2 * SSM_GROUP) ** -0.5),
        "ssm_b_im": nrm(ks[9], (DEPTH, SSM_GROUPS, SSM_STATE, SSM_GROUP), (2 * SSM_GROUP) ** -0.5),
        "ssm_c_re": nrm(ks[10], (DEPTH, SSM_GROUPS, SSM_GROUP, SSM_STATE), (2 * SSM_STATE) ** -0.5),
        "ssm_c_im": nrm(ks[11], (DEPTH, SSM_GROUPS, SSM_GROUP, SSM_STATE), (2 * SSM_STATE) ** -0.5),
        "ssm_d": nrm(ks[12], (DEPTH, SSM_WIDTH), 1.0),
        "ssm_w_glu": nrm(ks[13], (DEPTH, SSM_WIDTH, 2 * SSM_WIDTH), SSM_WIDTH ** -0.5),
        "ssm_w_out": nrm(ks[14], (DEPTH, SSM_WIDTH, D_MODEL), SSM_WIDTH ** -0.5),
        "mem_w_kv": nrm(ks[15], (DEPTH, D_MODEL, 2 * MEM_WIDTH), D_MODEL ** -0.5),
        "mem_w_out": nrm(ks[16], (DEPTH, MEM_WIDTH, D_MODEL), MEM_WIDTH ** -0.5),
        "w_o": nrm(ks[17], (DEPTH, D_MODEL, D_MODEL), DN_BETA * D_MODEL ** -0.5),
        "ln1_g": 1.0 + nrm(ks[18], (DEPTH, D_MODEL), 0.02),
        "ln1_b": nrm(ks[19], (DEPTH, D_MODEL), 0.02),
        "ffn_w_gate_up": nrm(ks[20], (DEPTH, D_MODEL, 2 * D_FF), D_MODEL ** -0.5),
        "ffn_w_down": nrm(ks[21], (DEPTH, D_FF, D_MODEL), DN_BETA * D_FF ** -0.5),
        "ln2_g": 1.0 + nrm(ks[22], (DEPTH, D_MODEL), 0.02),
        "ln2_b": nrm(ks[23], (DEPTH, D_MODEL), 0.02),
    }

def reference(x, mem, w_in, b_in, sb_w_out, ssm_lambda_re, ssm_lambda_im, ssm_log_dt,
              ssm_b_re, ssm_b_im, ssm_c_re, ssm_c_im, ssm_d, ssm_w_glu, ssm_w_out,
              mem_w_kv, mem_w_out, w_o, ln1_g, ln1_b, ffn_w_gate_up, ffn_w_down,
              ln2_g, ln2_b):
    bsz, seq, _ = x.shape
    splits = [SB_WIDTH, 2 * SB_WIDTH, 3 * SB_WIDTH,
              3 * SB_WIDTH + SSM_WIDTH, 3 * SB_WIDTH + SSM_WIDTH + MEM_WIDTH]
    for l in range(DEPTH):
        proj = jnp.einsum('bld,de->ble', x, w_in[l]) + b_in[l]
        q_sb, k_sb, v_sb, u_ssm, q_mem, gate_logits = jnp.split(proj, splits, axis=-1)

        hs = (bsz, seq, SB_HEADS, SB_HEAD_DIM)
        sb = _stick_breaking_attention(q_sb.reshape(hs), k_sb.reshape(hs), v_sb.reshape(hs))
        p_sb = jnp.einsum('ble,ed->bld', sb.reshape(bsz, seq, SB_WIDTH), sb_w_out[l])

        y = _s5(u_ssm, ssm_lambda_re[l], ssm_lambda_im[l], ssm_log_dt[l], ssm_b_re[l], ssm_b_im[l],
                ssm_c_re[l], ssm_c_im[l], ssm_d[l])
        g = jax.nn.gelu(y).astype(x.dtype)
        glu_a, glu_b = jnp.split(jnp.einsum('ble,ef->blf', g, ssm_w_glu[l]), 2, axis=-1)
        p_ssm = jnp.einsum('ble,ed->bld', glu_a * jax.nn.sigmoid(glu_b), ssm_w_out[l])

        mm = _memory_attention(q_mem, mem, mem_w_kv[l])
        p_mem = jnp.einsum('ble,ed->bld', mm, mem_w_out[l])

        gates = jax.nn.sigmoid(gate_logits.astype(jnp.float32)).astype(x.dtype)
        gates = gates.reshape(bsz, seq, N_BRANCHES, D_MODEL)
        merged = gates[:, :, 0] * p_sb + gates[:, :, 1] * p_ssm + gates[:, :, 2] * p_mem
        mix_out = jnp.einsum('bld,de->ble', merged, w_o[l])
        x = _layer_norm(DN_ALPHA * x + mix_out, ln1_g[l], ln1_b[l])

        gate_up = jnp.einsum('bld,df->blf', x, ffn_w_gate_up[l])
        f_gate, f_up = jnp.split(gate_up, 2, axis=-1)
        ffn_out = jnp.einsum('blf,fd->bld', jax.nn.silu(f_gate) * f_up, ffn_w_down[l])
        x = _layer_norm(DN_ALPHA * x + ffn_out, ln2_g[l], ln2_b[l])
    return x


_drawn_inputs = setup_inputs


def setup_inputs(seed=0):
    import zlib

    import numpy as np

    out = dict(_drawn_inputs(seed))
    spreads = {}
    factors = {'b_in': 8.0,
     'ssm_lambda_re': 64.0,
     'ssm_lambda_im': 64.0,
     'ssm_log_dt': 64.0,
     'ssm_b_re': 64.0,
     'ssm_b_im': 64.0,
     'ssm_c_re': 64.0,
     'ssm_c_im': 64.0}
    for name, (base, spread) in spreads.items():
        noise = np.random.default_rng([zlib.crc32(name.encode()), seed]).standard_normal(out[name].shape)
        drawn = base * np.exp(spread * noise) if base else spread * noise
        out[name] = __import__('jax').numpy.asarray(drawn.astype(out[name].dtype))
    for name, factor in factors.items():
        out[name] = (out[name] * factor).astype(out[name].dtype)
    return out
```

```python
from contextlib import ExitStack

import numpy as np

import concourse.bass as bass
from concourse import mybir

F32 = mybir.dt.float32
F32R = mybir.dt.float32r
BF16 = mybir.dt.bfloat16
I32 = mybir.dt.int32
ACT = mybir.ActivationFunctionType
ALU = mybir.AluOpType
AX_X = mybir.AxisListType.X

P = 128
T = 256
TT = T // P
D = 2048
KD = D // P
DEPTH = 2
HEADS = 8
SBW = HEADS * P
SSMW = 512
GROUPS = 32
STATE = 64
GC = 16
MEMW = 512
IN_W = 3 * SBW + SSMW + MEMW + 3 * D
D_FF = 5632
SCALE = float(P) ** -0.5
ALPHA = float((2 * DEPTH) ** 0.25)
EPS = 1e-5

CHUNK = 2048
HALF = CHUNK // 2
RAWS = 4
HLS = 4

PHASES = {
    "BR": (4, [0, 1, 2, 3, 0, 1, 2, 3, 0, 1], [4] + [1] * 9),
    "GLU": (1, [0, 1], [4, 4]),
    "G": (16, [0, 1, 2, 3], [1, 3, 1, 1]),
    "WO": (2, [0, 1, 2, 3] * 2, [1] * 8),
    "FF": (11, [0, 1, 2, 3] * 3, [1] * 12),
}
ORDER = ["BR", "GLU", "G", "WO", "FF"]
TILES = {"BR": 10, "GLU": 8, "G": 6, "WO": 0, "FF": 8}


def _bases(per_turn):
    base, total = {}, 0
    for ph in ORDER:
        base[ph] = total
        total += PHASES[ph][0] * per_turn[ph]
    return base, total


CH_BASE, CH_LAYER = _bases({ph: len(PHASES[ph][1]) for ph in ORDER})
TILE_BASE, TILE_LAYER = _bases(TILES)
FILL_BASE = {s: _bases({ph: sum(d for q, d in zip(*PHASES[ph][1:]) if q == s) for ph in ORDER})
             for s in range(RAWS)}
CH_ALL = DEPTH * CH_LAYER


def chunk_no(ph, l, i, c):
    return i * len(PHASES[ph][1]) + (l * CH_LAYER + CH_BASE[ph] + c)


def tile_no(ph, l, i, k):
    return i * TILES[ph] + (l * TILE_LAYER + TILE_BASE[ph] + k)


def filled(ph, l, i, c):
    _, slots, dmas = PHASES[ph]
    s = slots[c]
    base, total = FILL_BASE[s]
    per = sum(d for q, d in zip(slots, dmas) if q == s)
    upto = sum(d for q, d in zip(slots[:c + 1], dmas) if q == s)
    return i * (16 * per) + 16 * (l * total + base[ph] + upto)


def reuse_distance(ph, c):
    _, slots, _ = PHASES[ph]
    own = [c - k for k in range(c) if slots[k] == slots[c]]
    if own:
        return min(own)
    before = PHASES[ORDER[ORDER.index(ph) - 1]][1]
    wrap = [len(slots) - k + c for k in range(len(slots)) if slots[k] == slots[c]]
    enter = [len(before) - k + c for k in range(len(before)) if before[k] == slots[c]]
    return min(wrap + enter + [4])


HALF_CREDIT = HLS
TILE_CREDIT = 2
ROWS_CREDIT = 4

LN_STEPS = 13
GATES = ((0, 0, 0), (1, 2, 4), (2, 3, 5))
SCAN_STEPS = 10


def trunk(nc, x, mem, w_in, b_in, sb_w_out, lam_re_d, lam_im_d, log_dt_d, b_re_d, b_im_d, c_re_d,
          c_im_d, ssm_d, w_glu, ssm_w_out, w_kv, mem_w_out, w_o, ln1_g, ln1_b, w_gu, w_down,
          ln2_g, ln2_b, out):
    ctx = ExitStack()
    with ctx:
        def sb(name, shape, dt=F32, stack=ctx):
            return stack.enter_context(nc.sbuf_tensor(name, shape, dt))

        def sem(name):
            return ctx.enter_context(nc.semaphore(name))

        memT_save = nc.dram_tensor("memT_save", (P, KD * 2 * T), F32, kind="Internal").ap()
        tab_save = nc.dram_tensor("tab_save", (DEPTH * 4, P, 4 * P), F32, kind="Internal").ap()

        raw = sb("raw", [P, RAWS, CHUNK])
        hi = sb("hi", [P, HLS, HALF], F32R)
        lo = sb("lo", [P, HLS, HALF], F32R)
        xs = sb("xs", [P, KD, 2 * T], F32R)
        mT = sb("mT", [P, KD, 2 * T], F32R)
        rows = sb("rows", [P, TT, D])
        tmp = sb("tmp", [P, 2, T])

        region = ExitStack()
        sbT = sb("sbT", [P, HEADS, 2 * T], F32R, region)
        mmT = sb("mmT", [P, 4, 2 * T], F32R, region)
        gT = sb("gT", [P, 4, 2 * T], F32R, region)
        region.close()
        region = ExitStack()
        b_nat = sb("b_nat", [P, 2, 32, GC], stack=region)
        b_bar = sb("b_bar", [P, 4, 32, GC], stack=region)
        c_nat = sb("c_nat", [P, 2, 8, STATE], stack=region)
        b_blk = sb("b_blk", [P, 2, 8, P], stack=region)
        c_blk = sb("c_blk", [P, 2, 8, P], stack=region)
        region.close()
        hold_a = sb("hold_a", [P, 16 * 2 * T])

        region = ExitStack()
        scan = sb("scan", [P, 4, 2, T], stack=region)
        blocks = sb("blocks", [P, 2, 2, 32 + T // 4], stack=region)
        scan_t = sb("scan_t", [P, 2, T // 2], stack=region)
        region.close()
        region = ExitStack()
        ssmT = sb("ssmT", [P, 4, 2 * T], F32R, region)
        region.close()
        hold_b = sb("hold_b", [P, 2816])

        region = ExitStack()
        u_f = sb("u_f", [P, T], stack=region)
        q_f = sb("q_f", [P, T], stack=region)
        k_f = sb("k_f", [P, T], stack=region)
        v_f = sb("v_f", [P, T], stack=region)
        qm_f = sb("qm_f", [P, T], stack=region)
        km_f = sb("km_f", [P, T], stack=region)
        vm_f = sb("vm_f", [P, T], stack=region)
        v_s = sb("v_s", [P, 2, P], stack=region)
        vm_s = sb("vm_s", [P, 2, P], stack=region)
        soft = sb("soft", [P, 384], stack=region)
        sp_t = sb("sp_t", [P, 384], stack=region)
        w_t = sb("w_t", [P, 384], stack=region)
        prob = sb("prob", [P, 2, T], stack=region)
        probT = sb("probT", [P, 2, T], stack=region)
        gel_y = sb("gel_y", [P, T], stack=region)
        gel_t = sb("gel_t", [P, T], stack=region)
        region.close()
        region = ExitStack()
        mem_rows = sb("mem_rows", [P, TT, D], stack=region)
        sc = sb("sc", [P, 24, 32], stack=region)
        sci = sb("sci", [P, 3, 32], I32, region)
        region.close()
        region = ExitStack()
        gate = sb("gate", [P, 3, T], stack=region)
        bran = sb("bran", [P, 3, T], stack=region)
        acc = sb("acc", [P, T], stack=region)
        part = sb("part", [P, T], stack=region)
        region.close()
        region = ExitStack()
        gg = sb("gg", [P, 2, T], stack=region)
        th = sb("th", [P, 2, T], stack=region)
        uu = sb("uu", [P, 2, T], stack=region)
        hh = sb("hh", [P, 2, T], stack=region)
        region.close()
        region = ExitStack()
        xf = sb("xf", [P, 4, T], stack=region)
        region.close()
        hold_c = sb("hold_c", [P, 5120])

        tab = sb("tab", [P, 2, 4, P])
        par_nat = sb("par_nat", [P, 3, P])
        par = sb("par", [P, 3, P])
        qb_s = sb("qb_s", [P, DEPTH, HEADS])
        ident = sb("ident", [P, P])
        ident_r = sb("ident_r", [P, P], F32R)
        ident_b = sb("ident_b", [P, P], BF16)
        ntri = sb("ntri", [P, P])
        nones = sb("nones", [P, P])
        causal = sb("causal", [P, P])
        nbig = sb("nbig", [P, P], BF16)
        powers = sb("powers", [P, 24, 32])
        pw = sb("pw", [P, 24, 4])
        sm = sb("sm", [P, 8])
        st = sb("st", [P, TT, 4, 6])
        mv = sb("mv", [P, TT, 2])
        rv = sb("rv", [P, 4, TT])
        odd = sb("odd", [P, 4])
        oddi = sb("oddi", [P, 1], I32)

        bank = [ctx.enter_context(nc.psum_tensor(f"bank{b}", [P, 512], F32)) for b in range(8)]
        BU, Z, S, VO, Y = (bank[2], bank[3]), bank[4], bank[5], bank[6], bank[7]

        raw_full = [sem(f"raw_full{s}") for s in range(RAWS)]
        hi_ready, lo_ready, half_done = sem("hi_ready"), sem("lo_ready"), sem("half_done")
        first_out, tile_out, rows_out = sem("first_out"), sem("tile_out"), sem("rows_out")
        x_in, mem_in, par_in, ssm_in = sem("x_in"), sem("mem_in"), sem("par_in"), sem("ssm_in")
        masks, consts = sem("masks"), sem("consts")
        par_T, par_out = sem("par_T"), sem("par_out")
        init_T, init_hi, init_lo = sem("init_T"), sem("init_hi"), sem("init_lo")
        setup = sem("setup")
        tab_T, tab_out = sem("tab_T"), sem("tab_out")
        tab_saved = [sem("tab_saved0"), sem("tab_saved1")]
        memT_saved, memT_full, tab_full = sem("memT_saved"), sem("memT_full"), sem("tab_full")
        pw_ready, pads = sem("pw_ready"), sem("pads")
        bu_done, bu_copied, ks_step, y_done = sem("bu_done"), sem("bu_copied"), sem("ks_step"), sem("y_done")
        gelu_step, gelu_act = sem("gelu_step"), sem("gelu_act")
        z_done, soft_act, sp_step, tri_done, w_ready = (sem("z_done"), sem("soft_act"), sem("sp_step"),
                                                        sem("tri_done"), sem("w_ready"))
        vt_done, v_copied, attn_done = sem("vt_done"), sem("v_copied"), sem("attn_done")
        s_done, sm_step, p_exp = sem("s_done"), sem("sm_step"), sem("p_exp")
        pt_done, pt_copied, o_hi, o_lo = sem("pt_done"), sem("pt_copied"), sem("o_hi"), sem("o_lo")
        glu_th, glu_m, glu_hi, glu_lo = sem("glu_th"), sem("glu_m"), sem("glu_hi"), sem("glu_lo")
        gate_th, merge_step, merge_hi, merge_lo = (sem("gate_th"), sem("merge_step"), sem("merge_hi"),
                                                   sem("merge_lo"))
        stats_done, ln_step, norm_done, ln_T = sem("stats_done"), sem("ln_step"), sem("norm_done"), sem("ln_T")
        aff_dve, aff_act, xs_hi, xs_lo = sem("aff_dve"), sem("aff_act"), sem("xs_hi"), sem("xs_lo")
        rebuilt, resid_act, resid_dve = sem("rebuilt"), sem("resid_act"), sem("resid_dve")
        ffn_th, ffn_step, ffn_hi, ffn_lo = sem("ffn_th"), sem("ffn_step"), sem("ffn_hi"), sem("ffn_lo")
        gb_in, affine_rows, stored = sem("gb_in"), sem("affine_rows"), sem("stored")

        def bias_col(l, tile):
            return par[:, l, bass.ds(tile, 1)]

        def norm_cols(l, which, k):
            if which == 0:
                return par[:, l, 80 + k:81 + k], par[:, l, 96 + k:97 + k]
            return par[:, 2, 32 * l + k:32 * l + k + 1], par[:, 2, 32 * l + 16 + k:32 * l + 17 + k]

        def rows_no(ph, l, i, n, m):
            return (l * 96 + (8 if ph == "FF" else 0) + 2 * n + m) + i * (8 if ph == "FF" else 4)

        def next_chunk(ph, l, i, c):
            if c + 1 < len(PHASES[ph][1]):
                return ph, l, i, c + 1
            if PHASES[ph][0] > 1:
                return ph, l, i + 1, 0
            return ORDER[ORDER.index(ph) + 1], l, 0, 0

        block = ctx.enter_context(nc.Block())

        @block.sync
        def _(sp):
            sp.dma_start(rows[:], x.rearrange("b (m p) d -> p (b m) d", p=P)).then_inc(x_in, 16)
            for l in range(DEPTH):
                for src, at, n in ((b_in[l], 0, 80), (ln1_g[l], 80, 16), (ln1_b[l], 96, 16),
                                   (ssm_d[l], 112, 4)):
                    sp.dma_start(par_nat[at:at + n, l, :], src.rearrange("(n c) -> n c", c=P)).then_inc(par_in, 16)
                for src, at in ((ln2_g[l], 0), (ln2_b[l], 16)):
                    sp.dma_start(par_nat[32 * l + at:32 * l + at + 16, 2, :],
                                 src.rearrange("(n c) -> n c", c=P)).then_inc(par_in, 16)
            sp.dma_start(mem_rows[:], mem.rearrange("b (m p) d -> p (b m) d", p=P)).then_inc(mem_in, 16)

            def load(ph, l, i, c, pieces):
                g = chunk_no(ph, l, i, c)
                sp.wait_ge(lo_ready, g * 2 + (HALF_CREDIT + 2 - 2 * reuse_distance(ph, c)))
                slot = PHASES[ph][1][c]
                for dst, src in pieces(raw[:, slot, :]):
                    sp.dma_start(dst, src).then_inc(raw_full[slot], 16)

            def columns(w, col, parts=1):
                view = w.rearrange("(k p) n -> p k n", p=P)
                return lambda r: [(r.rearrange("p (k n) -> p k n", n=P)[:, k:k + KD // parts, :],
                                   view[:, k:k + KD // parts, bass.ds(col, P)]) for k in range(0, KD, KD // parts)]

            for l in range(DEPTH):
                with sp.Fori(0, 4) as i:
                    w = w_in[l]
                    cols = [(w, (i + 3 * SBW // P) * P), (w, (i + (3 * SBW + SSMW) // P) * P), (w_kv[l], i * P),
                            (w, i * 256), (w, i * 256 + SBW), (w, i * 256 + 2 * SBW),
                            (w, i * 256 + P), (w, i * 256 + SBW + P), (w, i * 256 + 2 * SBW + P),
                            (w_kv[l], i * P + MEMW)]
                    for c, (src, col) in enumerate(cols):
                        load("BR", l, i, c, columns(src, col, PHASES["BR"][2][c]))
                for c in range(2):
                    gv = w_glu[l].rearrange("(k p) (ab t n) -> t p k ab n", p=P, ab=2, n=P)

                    def pieces(r, c=c, gv=gv):
                        rr = r.rearrange("p (t k ab n) -> p t k ab n", t=2, k=4, ab=2)
                        return [(rr[:, t, :, ab], gv[2 * c + t][:, :, ab]) for t in range(2) for ab in range(2)]
                    load("GLU", l, 0, c, pieces)
                with sp.Fori(0, 16) as i:
                    def load_gate(b, c):
                        load("G", l, i, c, columns(w_in[l], (i + (3 * SBW + SSMW + MEMW + b * D) // P) * P))

                    def pieces(r):
                        rr = r.rearrange("p (k n) -> p k n", n=P)
                        at, got = 0, []
                        for w in (sb_w_out[l], ssm_w_out[l], mem_w_out[l]):
                            v = w.rearrange("(k p) n -> p k n", p=P)
                            k = v.shape[1]
                            got.append((rr[:, at:at + k, :], v[:, :, bass.ds(i * P, P)]))
                            at += k
                        return got
                    load_gate(0, 0)
                    load("G", l, i, 1, pieces)
                    load_gate(1, 2)
                    load_gate(2, 3)

                def block_rows(w, k0, col, n=4):
                    v = w.rearrange("(k p) n -> p k n", p=P)
                    return lambda r: [(r.rearrange("p (k n) -> p k n", n=512), v[:, k0, col])]

                with sp.Fori(0, 2) as i:
                    for c in range(8):
                        load("WO", l, i, c, block_rows(w_o[l], slice(4 * (c % 4), 4 * (c % 4) + 4),
                                                       bass.ds(i * 1024 + 512 * (c // 4), 512)))
                with sp.Fori(0, 11) as i:
                    for f in range(4):
                        load("FF", l, i, 2 * f, columns(w_gu[l], i * 512 + f * P))
                        load("FF", l, i, 2 * f + 1, columns(w_gu[l], i * 512 + (D_FF + f * P)))
                    for n in range(4):
                        load("FF", l, i, 8 + n, block_rows(w_down[l], bass.ds(i * 4, 4),
                                                           slice(512 * n, 512 * n + 512)))
            sp.wait_ge(lo_ready, 2 * CH_ALL + HALF_CREDIT)
            for j, v in enumerate((ln2_g[DEPTH - 1], ln2_b[DEPTH - 1])):
                sp.dma_start(raw[:, j, :], bass.AP(tensor=v.tensor, offset=v.offset, ap=[[0, P], [1, D]])
                             ).then_inc(gb_in, 16)
            for m in range(TT):
                sp.wait_ge(affine_rows, 8 * m + 8)
                sp.dma_start(out[0, m * P:(m + 1) * P, :], rows[:, m, :]).then_inc(stored, 16)
            sp.wait_ge(stored, 16 * TT)

        @block.gpsimd
        def _(pool):
            pool.memset(ident[:], 0.0).then_inc(masks, 1)
            pool.memset(ntri[:], -1.0).then_inc(masks, 1)
            pool.memset(nones[:], -1.0).then_inc(masks, 1)
            pool.memset(causal[:], 1.0).then_inc(masks, 1)
            pool.memset(nbig[:], -1e30).then_inc(masks, 1)
            pool.iota(oddi[:], pattern=[[0, 1]], base=0, channel_multiplier=1).then_inc(masks, 1)
            pool.wait_ge(masks, 6)
            pool.affine_select(out=ident[:], in_=ident[:], compare_op=ALU.not_equal, fill=1.0, base=0,
                               pattern=[[-1, P]], channel_multiplier=1).then_inc(masks, 1)
            pool.affine_select(out=ntri[:], in_=ntri[:], compare_op=ALU.is_ge, fill=0.0, base=0,
                               pattern=[[-1, P]], channel_multiplier=1).then_inc(masks, 1)
            pool.affine_select(out=causal[:], in_=causal[:], compare_op=ALU.is_gt, fill=0.0, base=0,
                               pattern=[[1, P]], channel_multiplier=-1).then_inc(masks, 1)
            pool.affine_select(out=nbig[:], in_=nbig[:], compare_op=ALU.is_ge, fill=0.0, base=0,
                               pattern=[[-1, P]], channel_multiplier=1).then_inc(masks, 1)

        @block.scalar
        def _(act):
            def hi_half(ph, l, i, c, h):
                slot = PHASES[ph][1][c]
                gh = chunk_no(ph, l, i, c) * 2 + h
                if h == 0:
                    act.wait_ge(raw_full[slot], filled(ph, l, i, c))
                act.wait_ge(half_done, gh + 1)
                act.activation(hi[:, hl_slot(ph, c, h), :],
                               raw[:, slot, h * HALF:(h + 1) * HALF], ACT.Copy).then_inc(hi_ready, 1)

            def split_next(ph, l, i, c):
                nxt = next_chunk(ph, l, i, c)
                for h in range(2):
                    if nxt[3] == 0:
                        slot = PHASES[nxt[0]][1][0]
                        gh = chunk_no(ph, l, i, c) * 2 + 2 + h
                        if h == 0:
                            act.wait_ge(raw_full[slot], filled(*nxt))
                        act.wait_ge(half_done, gh + 1)
                        act.activation(hi[:, hl_slot(ph, c + 1, h), :], raw[:, slot, h * HALF:(h + 1) * HALF],
                                       ACT.Copy).then_inc(hi_ready, 1)
                    else:
                        hi_half(ph, l, i, c + 1, h)

            def first_half(ph, l, i, k, src, ready, bias=None, scale=1.0):
                t = tile_no(ph, l, i, k)
                act.wait_ge(half_done, ready)
                act.wait_ge(tile_out, t + 1)
                if bias is None:
                    ins = act.activation(tmp[:, k % 2, :], src[:, 0:T], ACT.Copy, scale=scale)
                else:
                    ins = act.activation(tmp[:, k % 2, :], src[:, 0:T], ACT.Identity, bias=bias, scale=scale)
                ins.then_inc(first_out, 1)

            def done(ph, l, i, c, h=1):
                return chunk_no(ph, l, i, c) * 2 + (h + 1 + HALF_CREDIT)

            for l in range(DEPTH):
                for j, d in enumerate((lam_re_d, lam_im_d)):
                    act.dma_start(sc[:, j, 16 * l:16 * l + 16],
                                  d[l].rearrange("(j g) p -> (g p) j", g=2), allow_slow_non_contiguous=True).then_inc(ssm_in, 16)
                for g2 in range(2):
                    v = log_dt_d[l]
                    act.dma_start(sc[64 * g2:64 * g2 + 64, 2, 16 * l:16 * l + 16],
                                  bass.AP(tensor=v.tensor, offset=v.offset + g2, ap=[[0, 64], [2, 16]]),
                                  allow_slow_non_contiguous=True).then_inc(ssm_in, 16)
                for j, d in enumerate((b_re_d, b_im_d)):
                    act.dma_start(b_nat[:, j, 16 * l:16 * l + 16, :],
                                  d[l].rearrange("(j g) p c -> (g p) j c", g=2)).then_inc(ssm_in, 16)
                for j, d in enumerate((c_re_d, c_im_d)):
                    act.dma_start(c_nat[:, j, 4 * l:4 * l + 4, :],
                                  d[l].rearrange("(q g) c p -> (g c) q p", g=8)).then_inc(ssm_in, 16)

            act.wait_ge(par_T, 1)
            act.activation(par[:, 0:2, 0:116], bank[0][:, 0:2 * P].rearrange("p (a c) -> p a c", a=2)[:, :, 0:116],
                           ACT.Copy).then_inc(par_out, 1)
            act.activation(par[:, 2, 0:64], bank[0][:, 2 * P:2 * P + 64], ACT.Copy).then_inc(par_out, 1)
            for k in range(2 * KD):
                dst = xs if k < KD else mT
                act.wait_ge(init_T, k + 1)
                act.activation(dst[:, k % KD, 0:T], bank[4 + k % 4][:, 0:T], ACT.Copy).then_inc(init_hi, 1)
                if k == KD:
                    for h in range(2):
                        hi_half("BR", 0, 0, 0, h)
            act.wait_ge(init_lo, 2 * KD)
            act.dma_start(memT_save, mT[:].rearrange("p k t -> p (k t)").bitcast(F32)).then_inc(memT_saved, 16)
            for q in range(8):
                act.wait_ge(tab_T, q + 1)
                if q >= 2:
                    act.wait_ge(tab_saved[q % 2], 16 * (q // 2))
                act.activation(tab[:, q % 2].rearrange("p a c -> p (a c)"), bank[q % 2][:, :], ACT.Copy
                               ).then_inc(tab_out, 1)
                act.wait_ge(tab_out, q + 1)
                act.dma_start(tab_save[q], tab[:, q % 2].rearrange("p a c -> p (a c)")
                              ).then_inc(tab_saved[q % 2], 16)
            for s in range(2):
                act.wait_ge(tab_saved[s], 64)

            def norm(l, which):
                v = 2 * l + which
                for k in range(KD):
                    g, b = norm_cols(l, which, k)
                    if k % 2:
                        act.wait_ge(ln_T, 16 * v + k + 1)
                        if k >= 4:
                            act.wait_ge(xs_lo, 16 * v + k - 3)
                        act.activation(xf[:, k % 4, :], bank[4 + k % 4][:, 0:T], ACT.Identity, bias=b, scale=g
                                       ).then_inc(aff_act, 1)
                        act.wait_ge(aff_act, 8 * v + k // 2 + 1)
                    else:
                        act.wait_ge(aff_dve, 8 * v + k // 2 + 1)
                    act.activation(xs[:, k, 0:T], xf[:, k % 4, :], ACT.Copy).then_inc(xs_hi, 1)
                for n in range(4):
                    act.wait_ge(rebuilt, 8 * v + 2 * n + 1)
                    act.activation(rows[:, 0, 512 * n:512 * n + 512], bank[2 * n][:, :], ACT.Copy, scale=ALPHA
                                   ).then_inc(resid_act, 1)

            for l in range(DEPTH):
                with act.Fori(0, 4) as i:
                    n = i + 4 * l

                    def tile(c, bias_tile=None, scale=1.0, bias=None):
                        if bias is None and bias_tile is not None:
                            bias = bias_col(l, bias_tile)
                        first_half("BR", l, i, c, bank[c % 2], done("BR", l, i, c), bias, scale)

                    def copy_bu(j):
                        act.wait_ge(bu_done, n * 4 + (j + 1))
                        act.wait_ge(y_done, n * 4 + (j + 1))
                        act.activation(scan[:, j],
                                       BU[j % 2][:, :].rearrange("p (r t) -> p r t", r=2), ACT.Copy
                                       ).then_inc(bu_copied, 1)

                    def softplus(e):
                        act.wait_ge(z_done, n * 2 + (e + 2))
                        act.wait_ge(sp_step, n * 4 + (2 * e + 1))
                        act.activation(soft[:], Z[:, 0:384], ACT.Abs).then_inc(soft_act, 1)
                        act.wait_ge(soft_act, n * 6 + (3 * e + 1))
                        act.activation(soft[:], soft[:], ACT.Exp, scale=-1.0).then_inc(soft_act, 1)
                        act.wait_ge(soft_act, n * 6 + (3 * e + 2))
                        act.activation(soft[:], soft[:], ACT.Ln, bias=1.0).then_inc(soft_act, 1)

                    def weights(e):
                        act.wait_ge(tri_done, n * 2 + (e + 2))
                        act.wait_ge(attn_done, n * 3 + (2, 4)[e])
                        act.activation(w_t[:], Z[:, 0:384], ACT.Exp).then_inc(w_ready, 1)

                    def copy_v(k, src, dst, freed):
                        act.wait_ge(vt_done, n * 3 + (k + 4))
                        act.wait_ge(attn_done, n * 3 + freed)
                        act.activation(dst[:].rearrange("p a c -> p (a c)"), src[:, 0:T], ACT.Copy
                                       ).then_inc(v_copied, 1)

                    def out_hi(k, src, dst):
                        act.wait_ge(attn_done, n * 3 + (k + 4))
                        act.activation(dst, src[:, T:2 * T], ACT.Copy).then_inc(o_hi, 1)

                    split_next("BR", l, i, 0)
                    act.wait_ge(y_done, n * 4 + 4)
                    act.dma_start(tab[:, 0].rearrange("p a c -> p (a c)"),
                                  tab_save.rearrange("q p c -> p q c")[:, bass.ds(n, 1), :]
                                  ).then_inc(tab_full, 16)
                    tile(0, i + 24)
                    split_next("BR", l, i, 1)
                    tile(1, i + 28)
                    split_next("BR", l, i, 2)
                    copy_bu(0)
                    copy_bu(1)
                    tile(2)
                    split_next("BR", l, i, 3)
                    copy_bu(2)
                    copy_bu(3)
                    tile(3, scale=SCALE, bias=qb_s[:, l, bass.ds(i * 2, 1)])
                    split_next("BR", l, i, 4)
                    for t in range(TT):
                        act.wait_ge(sm_step, n * 5 + 7)
                        act.wait_ge(pt_done, n + 1)
                        act.activation(prob[:, t, :], S[:, t * T:(t + 1) * T], ACT.Exp, bias=sm[:, 2 + t:3 + t],
                                       scale=SCALE, accum_out=sm[:, 4 + t:5 + t]).then_inc(p_exp, 1)
                    tile(4, i * 2 + 8)
                    split_next("BR", l, i, 5)
                    tile(5, i * 2 + 16)
                    split_next("BR", l, i, 6)
                    softplus(0)
                    act.wait_ge(pt_done, n + 2)
                    act.wait_ge(attn_done, n * 3 + 3)
                    act.activation(probT[:].rearrange("p a c -> p (a c)"), S[:, :], ACT.Copy).then_inc(pt_copied, 1)
                    tile(6, scale=SCALE, bias=qb_s[:, l, bass.ds(i * 2 + 1, 1)])
                    split_next("BR", l, i, 7)
                    weights(0)
                    copy_v(0, VO, v_s, 2)
                    tile(7, i * 2 + 9)
                    split_next("BR", l, i, 8)
                    out_hi(0, VO, sbT[:, bass.ds(i * 2, 1), 0:T])
                    tile(8, i * 2 + 17)
                    split_next("BR", l, i, 9)
                    softplus(1)
                    tile(9)
                    weights(1)
                    copy_v(1, VO, v_s, 4)
                    act.wait_ge(gelu_step, n * 5 + 8)
                    act.activation(gel_t[:], gel_t[:], ACT.Tanh, scale=0.7978845608028654).then_inc(gelu_act, 1)
                    copy_v(2, S, vm_s, 3)
                    out_hi(1, VO, sbT[:, bass.ds(i * 2 + 1, 1), 0:T])
                    act.wait_ge(gelu_step, n * 5 + 9)
                    act.activation(gT[:, bass.ds(i, 1), 0:T], gel_t[:], ACT.Copy, scale=0.5).then_inc(gelu_act, 1)
                    out_hi(2, S, mmT[:, bass.ds(i, 1), 0:T])
                for c in range(2):
                    split_next("GLU", l, 0, c)
                    for h in range(2):
                        t = 2 * c + h
                        for k in (2 * t, 2 * t + 1):
                            first_half("GLU", l, 0, k, bank[k % 4], done("GLU", l, 0, c, h))
                        act.wait_ge(tile_out, tile_no("GLU", l, 0, 2 * t + 1) + 1 + TILE_CREDIT)
                        act.activation(gate[:, 1, :], gate[:, 1, :], ACT.Tanh, scale=0.5).then_inc(glu_th, 1)
                        act.wait_ge(glu_m, 4 * l + t + 1)
                        act.activation(ssmT[:, t, 0:T], acc[:], ACT.Copy, scale=0.5).then_inc(glu_hi, 1)
                if l == 0:
                    act.wait_ge(memT_saved, 16)
                with act.Fori(0, 16) as i:
                    n = i + 16 * l
                    for b, c, k in GATES:
                        split_next("G", l, i, c)
                        first_half("G", l, i, k, bank[k], done("G", l, i, c), bias_col(l, i + (32 + 16 * b)))
                        act.wait_ge(tile_out, tile_no("G", l, i, k) + (1 + TILE_CREDIT))
                        act.activation(gate[:, b, :], gate[:, b, :], ACT.Tanh, scale=0.5).then_inc(gate_th, 1)
                        if b == 0:
                            split_next("G", l, i, 1)
                            for k in range(3):
                                first_half("G", l, i, 1 + k, bank[1 + k], done("G", l, i, 1, 0 if k == 0 else 1))
                    act.wait_ge(merge_step, n * 5 + 10)
                    act.activation(mT[:, bass.ds(i, 1), 0:T], acc[:], ACT.Copy, scale=0.5).then_inc(merge_hi, 1)
                with act.Fori(0, 2) as i:
                    for c in range(8):
                        split_next("WO", l, i, c)
                norm(l, 0)
                last_l = l == DEPTH - 1

                def ffn_turn(i, last):
                    n = i + 11 * l
                    for c in range(12):
                        if not (last and last_l and c == 11):
                            split_next("FF", l, i, c) if not (last and c == 11) else split_into_next_layer()
                        if c < 8:
                            f = c // 2
                            first_half("FF", l, i, c, bank[2 * (f % 2) + c % 2], done("FF", l, i, c))
                            if c % 2:
                                act.wait_ge(tile_out, tile_no("FF", l, i, c - 1) + (1 + TILE_CREDIT))
                                act.activation(th[:, f % 2, :], gg[:, f % 2, :], ACT.Tanh, scale=0.5
                                               ).then_inc(ffn_th, 1)
                                act.wait_ge(ffn_step, n * 8 + (2 * f + 2 + 4))
                                act.activation(mT[:, f, 0:T], hh[:, f % 2, :], ACT.Copy).then_inc(ffn_hi, 1)

                def split_into_next_layer():
                    for h in range(2):
                        hi_half("BR", l + 1, 0, 0, h)

                with act.Fori(0, 10) as i:
                    ffn_turn(i, False)
                ffn_turn(10, True)
                if not last_l:
                    act.wait_ge(half_done, done("FF", l, 10, 11))
                    act.dma_start(mT[:].rearrange("p k t -> p (k t)").bitcast(F32), memT_save).then_inc(memT_full, 16)
                    norm(l, 1)

        @block.vector
        def _(dve):
            dve.sem_inc(half_done, HALF_CREDIT)
            dve.sem_inc(lo_ready, HALF_CREDIT)
            dve.sem_inc(tile_out, TILE_CREDIT)
            dve.sem_inc(rows_out, ROWS_CREDIT)
            for s, v in ((y_done, 4), (bu_copied, 2), (ks_step, 1), (gelu_step, 5), (sp_step, 2), (tri_done, 1),
                         (attn_done, 3), (w_ready, 1), (v_copied, 1), (vt_done, 3), (z_done, 1), (s_done, 1),
                         (pt_copied, 1), (sm_step, 5), (pt_done, 1), (o_lo, 1), (merge_step, 5), (merge_lo, 1),
                         (ffn_step, 4), (ffn_lo, 2)):
                dve.sem_inc(s, v)
            dve.memset(b_blk[:].rearrange("p a q c -> p (a q c)"), 0.0).then_inc(consts, 1)
            dve.wait_ge(masks, 10)
            dve.tensor_copy(ident_r[:], ident[:]).then_inc(consts, 1)
            dve.tensor_copy(ident_b[:], ident[:]).then_inc(consts, 1)

            def lo_half(slot, s, h, gh):
                dve.wait_ge(hi_ready, gh + 1)
                dve.tensor_tensor(lo[:, s, :], raw[:, slot, h * HALF:(h + 1) * HALF], hi[:, s, :].bitcast(F32),
                                  ALU.subtract).then_inc(lo_ready, 1)

            def split_next(ph, l, i, c):
                nxt = next_chunk(ph, l, i, c)
                slot = PHASES[nxt[0]][1][nxt[3]]
                for h in range(2):
                    lo_half(slot, hl_slot(ph, c + 1, h), h, chunk_no(ph, l, i, c) * 2 + (2 + h))

            def take(ph, l, i, k, src, dst, scale=1.0):
                t = tile_no(ph, l, i, k)
                dve.wait_ge(first_out, t + 1)
                dve.scalar_tensor_tensor(out=dst, in0=src[:, T:2 * T], scalar=scale, in1=tmp[:, k % 2, :],
                                         op0=ALU.mult, op1=ALU.add).then_inc(tile_out, 1)

            for k in range(2 * KD):
                dst = xs if k < KD else mT
                dve.wait_ge(init_hi, k + 1)
                dve.tensor_tensor(dst[:, k % KD, T:2 * T], bank[4 + k % 4][:, 0:T],
                                  dst[:, k % KD, 0:T].bitcast(F32), ALU.subtract).then_inc(init_lo, 1)
                if k == KD:
                    for h in range(2):
                        lo_half(0, h, h, h)
            dve.wait_ge(init_T, KD)
            dve.tensor_scalar(rows[:], rows[:], ALPHA, None, ALU.mult).then_inc(consts, 1)

            step = [0]

            def link(ins):
                step[0] += 1
                ins.then_inc(setup, 1)
                dve.wait_ge(setup, step[0])

            def V(k):
                return sc[:, k, :]

            def ts(dst, a, s1, s2=None, op0=ALU.mult, op1=None):
                link(dve.tensor_scalar(dst, a, s1, s2, op0, op1) if op1 else dve.tensor_scalar(dst, a, s1, None, op0))

            def tt(dst, a, b, op):
                link(dve.tensor_tensor(dst, a, b, op))

            def stt(dst, a, s, b, op0, op1):
                link(dve.scalar_tensor_tensor(out=dst, in0=a, scalar=s, in1=b, op0=op0, op1=op1))

            MAGIC = 12582912.0

            def exp(dst, src, k, r):
                ts(V(r), V(src), -87.0, 88.7, ALU.max, ALU.min)
                ts(V(k), V(r), 1.4426950408889634, MAGIC, ALU.mult, ALU.add)
                ts(V(k), V(k), -MAGIC, None, ALU.add)
                stt(V(r), V(k), -0.693359375, V(r), ALU.mult, ALU.add)
                stt(V(r), V(k), 2.12194440e-4, V(r), ALU.mult, ALU.add)
                ts(V(dst), V(r), 1.0 / 5040)
                for c in (1.0 / 720, 1.0 / 120, 1.0 / 24, 1.0 / 6, 0.5, 1.0):
                    stt(V(dst), V(dst), c, V(r), ALU.add, ALU.mult)
                ts(sci[:, 0, :], V(k), 127.0, 8388608.0, ALU.add, ALU.mult)
                stt(V(dst), V(dst), 1.0, sci[:, 0, :].bitcast(F32), ALU.add, ALU.mult)

            dve.wait_ge(ssm_in, 16 * 16)
            dve.wait_ge(consts, 1)
            exp(3, 2, 4, 5)
            tt(V(6), V(0), V(3), ALU.mult)
            tt(V(7), V(1), V(3), ALU.mult)
            exp(8, 6, 4, 5)
            ts(V(4), V(7), 0.6366197723675814, MAGIC, ALU.mult, ALU.add)
            ts(V(4), V(4), -MAGIC, None, ALU.add)
            stt(V(5), V(4), -1.5703125, V(7), ALU.mult, ALU.add)
            stt(V(5), V(4), -4.837512969970703125e-4, V(5), ALU.mult, ALU.add)
            stt(V(5), V(4), -7.54978995489188216e-8, V(5), ALU.mult, ALU.add)
            tt(V(9), V(5), V(5), ALU.mult)
            ts(V(10), V(9), -1.9515295891e-4, 8.3321608736e-3, ALU.mult, ALU.add)
            tt(V(10), V(10), V(9), ALU.mult)
            stt(V(10), V(10), -1.6666654611e-1, V(9), ALU.add, ALU.mult)
            stt(V(10), V(10), 1.0, V(5), ALU.add, ALU.mult)
            ts(V(11), V(9), 2.443315711809948e-5, -1.388731625493765e-3, ALU.mult, ALU.add)
            tt(V(11), V(11), V(9), ALU.mult)
            stt(V(11), V(11), 4.166664568298827e-2, V(9), ALU.add, ALU.mult)
            stt(V(11), V(11), -0.5, V(9), ALU.add, ALU.mult)
            ts(V(11), V(11), 1.0, None, ALU.add)
            link(dve.tensor_copy(sci[:, 0, :], V(4)))
            link(dve.tensor_scalar(sci[:, 1, :], sci[:, 0, :], 1, None, ALU.bitwise_and))
            link(dve.tensor_copy(V(12), sci[:, 1, :]))
            link(dve.tensor_scalar(sci[:, 1, :], sci[:, 0, :], 2, None, ALU.bitwise_and))
            link(dve.tensor_copy(V(13), sci[:, 1, :]))
            ts(V(14), V(4), 1.0, None, ALU.add)
            link(dve.tensor_copy(sci[:, 0, :], V(14)))
            link(dve.tensor_scalar(sci[:, 1, :], sci[:, 0, :], 2, None, ALU.bitwise_and))
            link(dve.tensor_copy(V(14), sci[:, 1, :]))
            ts(V(15), V(12), -1.0, 1.0, ALU.mult, ALU.add)
            tt(V(16), V(10), V(15), ALU.mult)
            tt(V(17), V(11), V(12), ALU.mult)
            tt(V(16), V(16), V(17), ALU.add)
            tt(V(17), V(11), V(15), ALU.mult)
            tt(V(18), V(10), V(12), ALU.mult)
            tt(V(17), V(17), V(18), ALU.add)
            for k in (13, 14):
                ts(V(k), V(k), -1.0, 1.0, ALU.mult, ALU.add)
                tt(V(k + 3), V(k + 3), V(k), ALU.mult)
                tt(V(k + 3), V(k + 3), V(8), ALU.mult)
            link(dve.tensor_copy(powers[:, 0, :], V(17)))
            link(dve.tensor_copy(powers[:, 8, :], V(16)))
            for k in range(8):
                re, im = powers[:, k, :], powers[:, 8 + k, :]
                ts(powers[:, 16 + k, :], im, -1.0)
                if k < 7:
                    tt(V(4), re, re, ALU.mult)
                    tt(V(5), im, im, ALU.mult)
                    tt(powers[:, k + 1, :], V(4), V(5), ALU.subtract)
                    stt(powers[:, 9 + k, :], re, 2.0, im, ALU.mult, ALU.mult)
            ts(V(4), powers[:, 0, :], -1.0, None, ALU.add)
            tt(V(5), V(0), V(0), ALU.mult)
            tt(V(9), V(1), V(1), ALU.mult)
            tt(V(5), V(5), V(9), ALU.add)
            link(dve.reciprocal(V(5), V(5)))
            tt(V(9), V(4), V(0), ALU.mult)
            tt(V(10), powers[:, 8, :], V(1), ALU.mult)
            tt(V(9), V(9), V(10), ALU.add)
            tt(V(9), V(9), V(5), ALU.mult)
            tt(V(10), powers[:, 8, :], V(0), ALU.mult)
            tt(V(11), V(4), V(1), ALU.mult)
            tt(V(10), V(10), V(11), ALU.subtract)
            tt(V(10), V(10), V(5), ALU.mult)
            f_re = sc[:, 9:10, :].rearrange("p a j -> p j a").broadcast_to([P, 32, GC])
            f_im = sc[:, 10:11, :].rearrange("p a j -> p j a").broadcast_to([P, 32, GC])
            tt(b_bar[:, 0], b_nat[:, 0], f_re, ALU.mult)
            tt(b_bar[:, 1], b_nat[:, 1], f_im, ALU.mult)
            tt(b_bar[:, 2], b_nat[:, 1], f_re, ALU.mult)
            tt(b_bar[:, 3], b_nat[:, 0], f_im, ALU.mult)
            tt(b_bar[:, 0], b_bar[:, 0], b_bar[:, 1], ALU.subtract)
            tt(b_bar[:, 2], b_bar[:, 2], b_bar[:, 3], ALU.add)
            for r in range(2):
                for g2 in range(2):
                    v = b_blk[64 * g2:64 * g2 + 64, r].rearrange("p q (j c) -> p (q j) c", c=32)
                    link(dve.tensor_copy(v[:, :, GC * g2:GC * g2 + GC], b_bar[64 * g2:64 * g2 + 64, 2 * r]))
            link(dve.tensor_scalar(oddi[:], oddi[:], 4, 1, ALU.logical_shift_right, ALU.bitwise_and))
            link(dve.tensor_copy(odd[:, 0:1], oddi[:]))
            ts(odd[:, 1:2], odd[:, 0:1], -1.0, 1.0, ALU.mult, ALU.add)
            ts(odd[:, 2:4], odd[:, 0:2], -1.0)
            for r in range(2):
                for g2 in range(2):
                    which = 2 * r + (1 - g2)
                    ts(c_blk[:, r, :, 64 * g2:64 * g2 + 64], c_nat[:, r], odd[:, which:which + 1])
            dve.wait_ge(par_out, 2)
            for l in range(DEPTH):
                ts(qb_s[:, l, :], par[:, l, 0:HEADS], SCALE)

            def norm(l, which):
                v = 2 * l + which
                base = LN_STEPS * v
                k = [0]

                def lnk(ins):
                    k[0] += 1
                    ins.then_inc(ln_step, 1)
                    dve.wait_ge(ln_step, base + k[0])

                dve.wait_ge(stats_done, 8 * v + 8)
                for m in range(TT):
                    lnk(dve.bn_aggr(mv[:, m, :], st[:, m, :, :].rearrange("p a b -> p (a b)")))
                var, r, t, u = rv[:, 0, :], rv[:, 1, :], rv[:, 2, :], rv[:, 3, :]
                lnk(dve.tensor_scalar(var, mv[:, :, 1], EPS, None, ALU.add))
                lnk(dve.tensor_scalar(r.bitcast(I32), var.bitcast(I32), -0.5, float(0x5f3759df), ALU.mult, ALU.add))
                for _ in range(3):
                    lnk(dve.scalar_tensor_tensor(out=t, in0=r, scalar=-0.5, in1=r, op0=ALU.mult, op1=ALU.mult))
                    lnk(dve.tensor_tensor(u, t, var, ALU.mult))
                    lnk(dve.scalar_tensor_tensor(out=r, in0=u, scalar=1.5, in1=r, op0=ALU.add, op1=ALU.mult))
                assert k[0] == LN_STEPS
                for c in range(4):
                    for m in range(TT):
                        y = rows[:, m, 512 * c:512 * c + 512]
                        dve.tensor_scalar(y, y, mv[:, m, 0:1], rv[:, 1, m:m + 1], ALU.subtract, ALU.mult
                                          ).then_inc(norm_done, 1)
                if v == 2 * DEPTH - 1:
                    dve.wait_ge(gb_in, 32)
                    for m in range(TT):
                        for c in range(4):
                            y = rows[:, m, 512 * c:512 * c + 512]
                            w = slice(512 * c, 512 * c + 512)
                            at = 8 * m + 2 * c
                            dve.wait_ge(norm_done, 8 * v + 8)
                            dve.tensor_tensor(y, y, raw[:, 0, w], ALU.mult).then_inc(affine_rows, 1)
                            dve.wait_ge(affine_rows, at + 1)
                            dve.tensor_tensor(y, y, raw[:, 1, w], ALU.add).then_inc(affine_rows, 1)
                    return

                def affine(k):
                    g, b = norm_cols(l, which, k)
                    dve.wait_ge(ln_T, 16 * v + k + 1)
                    if k >= 4:
                        dve.wait_ge(xs_lo, 16 * v + k - 3)
                    dve.tensor_scalar(xf[:, k % 4, :], bank[4 + k % 4][:, 0:T], g, b, ALU.mult, ALU.add
                                      ).then_inc(aff_dve, 1)

                def lo_part(k):
                    dve.wait_ge(xs_hi, 16 * v + k + 1)
                    dve.tensor_tensor(xs[:, k, T:2 * T], xf[:, k % 4, :], xs[:, k, 0:T].bitcast(F32), ALU.subtract
                                      ).then_inc(xs_lo, 1)

                affine(0)
                for k in range(2, KD, 2):
                    affine(k)
                    lo_part(k - 2)
                    lo_part(k - 1)
                lo_part(KD - 2)
                lo_part(KD - 1)
                for nn in range(4):
                    dve.wait_ge(rebuilt, 8 * v + 2 * nn + 2)
                    dve.tensor_scalar(rows[:, 1, 512 * nn:512 * nn + 512], bank[2 * nn + 1][:, :], ALPHA, None,
                                      ALU.mult).then_inc(resid_dve, 1)

            def add_rows(ph, l, i, n, m, src, stats=None, ready=0, dyn=None):
                y = rows[:, m, 512 * n:512 * n + 512] if dyn is None else rows[:, m, bass.ds(dyn, 512)]
                dve.wait_ge(half_done, ready)
                dve.tensor_tensor(y, y, src[:, :], ALU.add).then_inc(rows_out, 1)
                if stats is not None:
                    dve.wait_ge(rows_out, rows_no(ph, l, i, n % 2 if ph == "WO" else n, m) + (1 + ROWS_CREDIT))
                    dve.bn_stats(stats, y).then_inc(stats_done, 1)

            for l in range(DEPTH):
                dve.memset(blocks[:].rearrange("p a r t -> p (a r) t")[:, :, 0:32], 0.0).then_inc(pads, 1)
                dve.wait_ge(pads, l + 1)
                with dve.Fori(0, 4) as i:
                    n = i + 4 * l

                    def tile(c, dst, scale=1.0):
                        take("BR", l, i, c, bank[c % 2], dst[:], scale)

                    def scan_states(j, first, last_):
                        X = scan[:, j]

                        def at_times(start, stride, count):
                            return X[:, :, start:start + stride * (count - 1) + 1:stride]

                        def sums(which, back):
                            return blocks[:, which, :, 32 - back:32 + T // 4 - back]

                        steps = [(0, at_times(0, 2, 128), at_times(1, 2, 128), at_times(1, 2, 128)),
                                 (1, at_times(1, 4, 64), at_times(3, 4, 64), sums(0, 0))]
                        for q in range(6):
                            steps.append((2 + q, sums(q % 2, 1 << q), sums(q % 2, 0),
                                          sums(1 - q % 2, 0) if q < 5 else at_times(3, 4, 64)))
                        steps += [(1, at_times(3, 4, 63), at_times(5, 4, 63), at_times(5, 4, 63)),
                                  (0, at_times(1, 2, 127), at_times(2, 2, 127), at_times(2, 2, 127))]
                        assert len(steps) == SCAN_STEPS
                        for q in range(first, last_):
                            lev, early, late, dst = steps[q]
                            count = early.shape[2]
                            at = n * (12 * SCAN_STEPS) + (3 * (SCAN_STEPS * j + q) + 1)
                            a_re, a_im, a_ni = (pw[:, 8 * r + lev, j:j + 1] for r in range(3))
                            if q == 0:
                                dve.wait_ge(bu_copied, n * 4 + (j + 3))
                            dve.wait_ge(ks_step, at)
                            dve.scalar_tensor_tensor(out=scan_t[:, :, 0:count], in0=early, scalar=a_re, in1=late,
                                                     op0=ALU.mult, op1=ALU.add).then_inc(ks_step, 1)
                            dve.wait_ge(ks_step, at + 1)
                            dve.scalar_tensor_tensor(out=dst[:, 0], in0=early[:, 1], scalar=a_ni,
                                                     in1=scan_t[:, 0, 0:count], op0=ALU.mult, op1=ALU.add
                                                     ).then_inc(ks_step, 1)
                            dve.scalar_tensor_tensor(out=dst[:, 1], in0=early[:, 0], scalar=a_im,
                                                     in1=scan_t[:, 1, 0:count], op0=ALU.mult, op1=ALU.add
                                                     ).then_inc(ks_step, 1)

                    def softplus(e):
                        dve.wait_ge(soft_act, n * 6 + (3 * e + 3))
                        dve.wait_ge(tri_done, n * 2 + (e + 1))
                        dve.scalar_tensor_tensor(out=sp_t[:], in0=Z[:, 0:384], scalar=0.0, in1=soft[:],
                                                 op0=ALU.max, op1=ALU.add).then_inc(sp_step, 1)
                        dve.wait_ge(sp_step, n * 4 + (2 * e + 3))
                        v = sp_t[:].rearrange("p (a c) -> p a c", a=3)[:, 0:3:2, :]
                        cm = causal[:].rearrange("p (a c) -> p a c", a=1).broadcast_to([P, 2, P])
                        dve.tensor_tensor(v, v, cm, ALU.mult).then_inc(sp_step, 1)

                    def out_lo(k, src, dst, hi_part):
                        dve.wait_ge(o_hi, n * 3 + (k + 1))
                        dve.tensor_tensor(dst, src[:, T:2 * T], hi_part.bitcast(F32), ALU.subtract).then_inc(o_lo, 1)

                    def part_of(t, k, lo_side):
                        return t[:, bass.ds(k, 1), T:2 * T] if lo_side else t[:, bass.ds(k, 1), 0:T]

                    dve.wait_ge(ks_step, n * (12 * SCAN_STEPS) + 1)
                    dve.tensor_copy(pw[:], powers[:, :, bass.ds(n * 4, 4)]).then_inc(pw_ready, 1)
                    split_next("BR", l, i, 0)
                    dve.wait_ge(gelu_step, n * 5 + 1)
                    tile(0, u_f)
                    split_next("BR", l, i, 1)
                    dve.wait_ge(s_done, n + 1)
                    tile(1, qm_f)
                    split_next("BR", l, i, 2)
                    dve.wait_ge(pw_ready, n + 1)
                    scan_states(0, 0, 5)
                    tile(2, km_f)
                    split_next("BR", l, i, 3)
                    scan_states(0, 5, 10)
                    dve.wait_ge(z_done, n * 2 + 1)
                    tile(3, q_f, SCALE)
                    split_next("BR", l, i, 4)
                    dve.wait_ge(s_done, n + 2)
                    dve.wait_ge(sm_step, n * 5 + 5)
                    dve.tensor_reduce(sm[:, 0:2], S[:, :].rearrange("p (a c) -> p a c", a=2), AX_X, ALU.max
                                      ).then_inc(sm_step, 1)
                    dve.wait_ge(sm_step, n * 5 + 6)
                    dve.tensor_scalar(sm[:, 2:4], sm[:, 0:2], -SCALE, None, ALU.mult).then_inc(sm_step, 1)
                    scan_states(1, 0, 5)
                    tile(4, k_f)
                    split_next("BR", l, i, 5)
                    dve.wait_ge(p_exp, n * 2 + 2)
                    dve.reciprocal(sm[:, 6:8], sm[:, 4:6]).then_inc(sm_step, 1)
                    dve.wait_ge(sm_step, n * 5 + 8)
                    for t in range(TT):
                        dve.tensor_scalar(prob[:, t, :], prob[:, t, :], sm[:, 6 + t:7 + t], None, ALU.mult
                                          ).then_inc(sm_step, 1)
                    scan_states(1, 5, 10)
                    dve.wait_ge(vt_done, n * 3 + 2)
                    tile(5, v_f)
                    split_next("BR", l, i, 6)
                    scan_states(2, 0, 5)
                    softplus(0)
                    dve.wait_ge(z_done, n * 2 + 2)
                    tile(6, q_f, SCALE)
                    split_next("BR", l, i, 7)
                    scan_states(2, 5, 10)
                    tile(7, k_f)
                    split_next("BR", l, i, 8)
                    scan_states(3, 0, 5)
                    out_lo(0, VO, part_of(sbT, i * 2, 1), part_of(sbT, i * 2, 0))
                    dve.wait_ge(vt_done, n * 3 + 4)
                    tile(8, v_f)
                    split_next("BR", l, i, 9)
                    scan_states(3, 5, 10)
                    softplus(1)
                    dve.wait_ge(vt_done, n * 3 + 3)
                    tile(9, vm_f)
                    dve.wait_ge(y_done, n * 4 + 8)
                    dve.wait_ge(gelu_step, n * 5 + 5)
                    dve.scalar_tensor_tensor(out=gel_y[:], in0=u_f[:], scalar=bias_col(l, i + 112), in1=Y[:, 0:T],
                                             op0=ALU.mult, op1=ALU.add).then_inc(gelu_step, 1)
                    dve.wait_ge(gelu_step, n * 5 + 6)
                    dve.scalar_tensor_tensor(out=gel_t[:], in0=gel_y[:], scalar=0.044715, in1=gel_y[:],
                                             op0=ALU.mult, op1=ALU.mult).then_inc(gelu_step, 1)
                    dve.wait_ge(gelu_step, n * 5 + 7)
                    dve.scalar_tensor_tensor(out=gel_t[:], in0=gel_t[:], scalar=1.0, in1=gel_y[:],
                                             op0=ALU.add, op1=ALU.mult).then_inc(gelu_step, 1)
                    dve.wait_ge(gelu_act, n * 2 + 1)
                    dve.scalar_tensor_tensor(out=gel_t[:], in0=gel_t[:], scalar=1.0, in1=gel_y[:],
                                             op0=ALU.add, op1=ALU.mult).then_inc(gelu_step, 1)
                    out_lo(1, VO, part_of(sbT, i * 2 + 1, 1), part_of(sbT, i * 2 + 1, 0))
                    dve.wait_ge(gelu_act, n * 2 + 2)
                    dve.scalar_tensor_tensor(out=part_of(gT, i, 1), in0=gel_t[:], scalar=0.5,
                                             in1=part_of(gT, i, 0).bitcast(F32), op0=ALU.mult,
                                             op1=ALU.subtract).then_inc(gelu_step, 1)
                    out_lo(2, S, part_of(mmT, i, 1), part_of(mmT, i, 0))
                for c in range(2):
                    split_next("GLU", l, 0, c)
                    for h in range(2):
                        t = 2 * c + h
                        if l + t > 0:
                            dve.wait_ge(glu_m, 4 * l + t)
                        for k in (2 * t, 2 * t + 1):
                            take("GLU", l, 0, k, bank[k % 4], gate[:, k % 2, :])
                        dve.wait_ge(glu_th, 4 * l + t + 1)
                        if l + t > 0:
                            dve.wait_ge(glu_lo, 4 * l + t)
                        dve.scalar_tensor_tensor(out=acc[:], in0=gate[:, 1, :], scalar=1.0, in1=gate[:, 0, :],
                                                 op0=ALU.add, op1=ALU.mult).then_inc(glu_m, 1)
                        dve.wait_ge(glu_hi, 4 * l + t + 1)
                        dve.scalar_tensor_tensor(out=ssmT[:, t, T:2 * T], in0=acc[:], scalar=0.5,
                                                 in1=ssmT[:, t, 0:T].bitcast(F32), op0=ALU.mult,
                                                 op1=ALU.subtract).then_inc(glu_lo, 1)
                dve.wait_ge(glu_lo, 4 * l + 4)
                with dve.Fori(0, 16) as i:
                    n = i + 16 * l
                    for b, c, k in GATES:
                        split_next("G", l, i, c)
                        if b == 0:
                            dve.wait_ge(merge_step, n * 5 + 5)
                        take("G", l, i, k, bank[k], gate[:, b, :])
                        if b == 0:
                            split_next("G", l, i, 1)
                            for k in range(3):
                                take("G", l, i, 1 + k, bank[1 + k], bran[:, k, :])
                            dve.wait_ge(tile_out, tile_no("G", l, i, 3) + (1 + TILE_CREDIT))
                        dve.wait_ge(gate_th, n * 3 + (b + 1))
                        if b == 0:
                            dve.wait_ge(merge_lo, n + 1)
                            dve.scalar_tensor_tensor(out=acc[:], in0=gate[:, 0, :], scalar=1.0, in1=bran[:, 0, :],
                                                     op0=ALU.add, op1=ALU.mult).then_inc(merge_step, 1)
                        else:
                            dve.wait_ge(merge_step, n * 5 + (2 * b - 1 + 5))
                            dve.scalar_tensor_tensor(out=part[:], in0=gate[:, b, :], scalar=1.0,
                                                     in1=bran[:, b, :], op0=ALU.add, op1=ALU.mult
                                                     ).then_inc(merge_step, 1)
                            dve.wait_ge(merge_step, n * 5 + (2 * b + 5))
                            dve.tensor_tensor(acc[:], acc[:], part[:], ALU.add).then_inc(merge_step, 1)
                    dve.wait_ge(merge_hi, n + 1)
                    dve.scalar_tensor_tensor(out=mT[:, bass.ds(i, 1), T:2 * T], in0=acc[:], scalar=0.5,
                                             in1=mT[:, bass.ds(i, 1), 0:T].bitcast(F32), op0=ALU.mult,
                                             op1=ALU.subtract).then_inc(merge_lo, 1)
                if l:
                    dve.wait_ge(resid_act, 4 * (2 * l - 1) + 4)
                    dve.wait_ge(resid_dve, 4 * (2 * l - 1) + 4)
                else:
                    dve.wait_ge(consts, 4)
                with dve.Fori(0, 2) as i:
                    for c in range(8):
                        split_next("WO", l, i, c)
                        if c % 4 == 3:
                            nn = c // 4
                            for m in range(TT):
                                add_rows("WO", l, i, nn, m, bank[6 - 2 * nn + m],
                                         stats=st[:, m, bass.ds(i * 2 + nn, 1), :],
                                         ready=chunk_no("WO", l, i, c) * 2 + (2 + HALF_CREDIT),
                                         dyn=i * 1024 + 512 * nn)
                norm(l, 0)
                last_l = l == DEPTH - 1

                def ffn_turn(i, last):
                    n = i + 11 * l
                    for c in range(12):
                        if last and c == 11:
                            if not last_l:
                                for h in range(2):
                                    lo_half(0, h, h, chunk_no("BR", l + 1, 0, 0) * 2 + h)
                        else:
                            split_next("FF", l, i, c)
                        if c < 8:
                            f = c // 2
                            b = bank[2 * (f % 2) + c % 2]
                            if c % 2 == 0:
                                dve.wait_ge(ffn_step, n * 8 + (2 * f + 1))
                                take("FF", l, i, c, b, gg[:, f % 2, :])
                            else:
                                dve.wait_ge(ffn_step, n * 8 + (2 * f + 2))
                                take("FF", l, i, c, b, uu[:, f % 2, :])
                                dve.wait_ge(ffn_th, n * 4 + (f + 1))
                                dve.wait_ge(ffn_lo, n * 4 + (f + 1))
                                dve.scalar_tensor_tensor(out=hh[:, f % 2, :], in0=th[:, f % 2, :], scalar=1.0,
                                                         in1=gg[:, f % 2, :], op0=ALU.add, op1=ALU.mult
                                                         ).then_inc(ffn_step, 1)
                                dve.wait_ge(ffn_step, n * 8 + (2 * f + 1 + 4))
                                dve.wait_ge(tile_out, tile_no("FF", l, i, c) + (1 + TILE_CREDIT))
                                dve.scalar_tensor_tensor(out=hh[:, f % 2, :], in0=hh[:, f % 2, :], scalar=0.5,
                                                         in1=uu[:, f % 2, :], op0=ALU.mult, op1=ALU.mult
                                                         ).then_inc(ffn_step, 1)
                                dve.wait_ge(ffn_hi, n * 4 + (f + 1))
                                dve.tensor_tensor(mT[:, f, T:2 * T], hh[:, f % 2, :], mT[:, f, 0:T].bitcast(F32),
                                                  ALU.subtract).then_inc(ffn_lo, 1)
                        else:
                            nn = c - 8
                            if nn == 0:
                                dve.wait_ge(resid_act, 4 * (2 * l) + 4)
                                dve.wait_ge(resid_dve, 4 * (2 * l) + 4)
                                dve.wait_ge(rows_out, rows_no("FF", l, i, 0, 0) + ROWS_CREDIT)
                            for m in range(TT):
                                add_rows("FF", l, i, nn, m, bank[6 - 2 * (nn % 2) + m],
                                         stats=st[:, m, nn, :] if last else None,
                                         ready=chunk_no("FF", l, i, c) * 2 + (2 + HALF_CREDIT))

                with dve.Fori(0, 10) as i:
                    ffn_turn(i, False)
                ffn_turn(10, True)
                norm(l, 1)

        @block.tensor
        def _(pe):
            def product(ph, l, i, c, h, dst, x_t, k0, first, last):
                gh = chunk_no(ph, l, i, c) * 2 + h
                s = hl_slot(ph, c, h)
                pe.wait_ge(lo_ready, gh + (1 + HALF_CREDIT))
                for k in range(8):
                    w = slice(k * P, (k + 1) * P)
                    pe.matmul(dst[:, :], hi[:, s, w], x_t[:, k0 + k, :], start=first and k == 0, stop=False)
                    ins = pe.matmul(dst[:, 0:T], lo[:, s, w], x_t[:, k0 + k, 0:T], start=False,
                                    stop=last and k == 7)
                ins.then_inc(half_done, 1)

            def rows_product(ph, l, i, c, h, k0, banks, first, last, ready=None):
                gh = chunk_no(ph, l, i, c) * 2 + h
                s = hl_slot(ph, c, h)
                pe.wait_ge(lo_ready, gh + (1 + HALF_CREDIT))
                for m in range(TT):
                    for k in range(2):
                        if ready is not None:
                            pe.wait_ge(*ready(k0 + k))
                        xh = mT[:, k0 + k, m * P:(m + 1) * P]
                        xl = mT[:, k0 + k, T + m * P:T + (m + 1) * P]
                        wh, wl = hi[:, s, k * 512:(k + 1) * 512], lo[:, s, k * 512:(k + 1) * 512]
                        pe.matmul(banks[m][:, :], xh, wh, start=first and k == 0, stop=False)
                        pe.matmul(banks[m][:, :], xh, wl, start=False, stop=False)
                        ins = pe.matmul(banks[m][:, :], xl, wh, start=False, stop=last and k == 1)
                ins.then_inc(half_done, 1)

            pe.wait_ge(masks, 10)
            pe.wait_ge(par_in, 16 * 12)
            for a, n in ((0, 116), (1, 116), (2, 64)):
                ins = pe.transpose(bank[0][:, a * P:a * P + n], par_nat[0:n, a, :], ident[0:n, 0:n])
            ins.then_inc(par_T, 1)
            for k in range(2 * KD):
                src = rows if k < KD else mem_rows
                if k == 0:
                    pe.wait_ge(x_in, 16)
                if k == KD:
                    pe.wait_ge(mem_in, 16)
                if k >= 4:
                    pe.wait_ge(init_lo, k - 3)
                for m in range(TT):
                    ins = pe.transpose(bank[4 + k % 4][:, m * P:(m + 1) * P],
                                       src[:, m, (k % KD) * P:(k % KD + 1) * P], ident[:])
                ins.then_inc(init_T, 1)
            pe.wait_ge(setup, SETUP_STEPS)
            pe.wait_ge(par_out, 2)
            for q in range(8):
                if q >= 2:
                    pe.wait_ge(tab_out, q - 1)
                for r in range(4):
                    src = (b_blk, c_blk)[r // 2][:, r % 2, q, :]
                    ins = pe.transpose(bank[q % 2][:, r * P:(r + 1) * P], src, ident[:])
                ins.then_inc(tab_T, 1)
            pe.wait_ge(tab_out, 8)
            pe.wait_ge(init_lo, 2 * KD)
            pe.wait_ge(consts, 3)

            def norm(l, which):
                v = 2 * l + which
                for k in range(KD):
                    pe.wait_ge(norm_done, 8 * v + 2 * (k // 4) + 2)
                    if k >= 4:
                        if k % 2:
                            pe.wait_ge(aff_act, 8 * v + (k - 4) // 2 + 1)
                        else:
                            pe.wait_ge(aff_dve, 8 * v + (k - 4) // 2 + 1)
                    for m in range(TT):
                        ins = pe.transpose(bank[4 + k % 4][:, m * P:(m + 1) * P], rows[:, m, k * P:(k + 1) * P],
                                           ident[:])
                    ins.then_inc(ln_T, 1)
                for n in range(4):
                    if n == 0:
                        ph = "FF" if which else "G"
                        pe.wait_ge(tile_out, tile_no(ph, l, PHASES[ph][0] - 1, TILES[ph] - 1) + 1 + TILE_CREDIT)
                    pe.wait_ge(xs_lo, 16 * v + (4 * n + 4 if n < 2 else 16))
                    for m in range(TT):
                        for k in range(4):
                            o = bank[2 * n + m][:, k * P:(k + 1) * P]
                            kk = 4 * n + k
                            pe.matmul(o, xs[:, kk, m * P:(m + 1) * P], ident_r[:], start=True, stop=False)
                            ins = pe.matmul(o, xs[:, kk, T + m * P:T + (m + 1) * P], ident_r[:], start=False,
                                            stop=True)
                        ins.then_inc(rebuilt, 1)

            for l in range(DEPTH):
                if l:
                    pe.wait_ge(resid_act, 4 * (2 * l - 1) + 4)
                    pe.wait_ge(resid_dve, 4 * (2 * l - 1) + 4)
                with pe.Fori(0, 4) as i:
                    n = i + 4 * l

                    def gemm(c, x_t):
                        pe.wait_ge(tile_out, tile_no("BR", l, i, c) + 1)
                        for h in range(2):
                            product("BR", l, i, c, h, bank[c % 2], x_t, 8 * h, h == 0, h == 1)

                    def got(c):
                        pe.wait_ge(tile_out, tile_no("BR", l, i, c) + (1 + TILE_CREDIT))

                    def bu(j):
                        pe.wait_ge(bu_copied, n * 4 + (j + 1))
                        r = slice(32 * j, 32 * j + 32)
                        for a in range(2):
                            ins = pe.matmul(BU[j % 2][:, a * T:(a + 1) * T], tab[r, 0, a, :], u_f[r, :],
                                            start=True, stop=True, tile_position=(32 * j, 0))
                        ins.then_inc(bu_done, 1)

                    def y_part(j):
                        pe.wait_ge(ks_step, n * (12 * SCAN_STEPS) + (3 * SCAN_STEPS * (j + 1) + 1))
                        if j == 0:
                            pe.wait_ge(gelu_step, n * 5 + 1)
                        r = slice(32 * j, 32 * j + 32)
                        for a in range(2):
                            ins = pe.matmul(Y[r, 0:T], tab[:, 0, 2 + a, r], scan[:, j, a, :],
                                            start=a == 0, stop=a == 1, tile_position=(0, 32 * j))
                        ins.then_inc(y_done, 1)

                    def z(e):
                        pe.wait_ge(w_ready, n * 2 + (e + 1))
                        pe.matmul(Z[:, 0:T], k_f[:, 0:P], q_f[:], start=True, stop=False, skip_group_check=True)
                        pe.matmul(Z[:, T:384], k_f[:, P:T], q_f[:, P:T], start=False, stop=False,
                                  skip_group_check=True).then_inc(z_done, 1)

                    def tri(e):
                        pe.wait_ge(sp_step, n * 4 + (2 * e + 4))
                        pe.matmul(Z[:, 0:T], ntri[:], sp_t[:, 0:T], start=False, stop=False, skip_group_check=True)
                        pe.matmul(Z[:, P:T], nones[:], sp_t[:, T:384], start=False, stop=False,
                                  skip_group_check=True)
                        pe.matmul(Z[:, T:384], ntri[:], sp_t[:, T:384], start=False, stop=False,
                                  skip_group_check=True)
                        pe.matmul(Z[:, 0:P], ident_b[:], nbig[:], start=False, stop=False, skip_group_check=True)
                        pe.matmul(Z[:, T:384], ident_b[:], nbig[:], start=False, stop=True,
                                  skip_group_check=True).then_inc(tri_done, 1)

                    def v_turn(k, src, o):
                        pe.wait_ge(v_copied, n * 3 + (k + 1))
                        for t in range(2):
                            ins = pe.transpose(o[:, t * P:(t + 1) * P], src[:, t * P:(t + 1) * P], ident[:])
                        ins.then_inc(vt_done, 1)

                    def attend(e):
                        pe.wait_ge(w_ready, n * 2 + (e + 2))
                        pe.wait_ge(v_copied, n * 3 + (e + 2))
                        pe.wait_ge(o_lo, n * 3 + (e + 1))
                        pe.matmul(VO[:, T:2 * T], v_s[:, 0, :], w_t[:, 0:T], start=True, stop=False)
                        pe.matmul(VO[:, T + P:2 * T], v_s[:, 1, :], w_t[:, T:384], start=False, stop=True
                                  ).then_inc(attn_done, 1)

                    gemm(0, xs)
                    gemm(1, xs)
                    pe.wait_ge(tab_full, n * 16 + 16)
                    got(0)
                    bu(0)
                    bu(1)
                    if l:
                        pe.wait_ge(memT_full, 16 * l)
                    gemm(2, mT)
                    bu(2)
                    bu(3)
                    gemm(3, xs)
                    got(2)
                    pe.wait_ge(pt_copied, n + 1)
                    pe.wait_ge(o_lo, n * 3 + 1)
                    for t in range(TT):
                        ins = pe.matmul(S[:, t * T:(t + 1) * T], qm_f[:, t * P:(t + 1) * P], km_f[:], start=True,
                                        stop=True)
                    ins.then_inc(s_done, 1)
                    gemm(4, xs)
                    gemm(5, xs)
                    got(4)
                    z(0)
                    pe.wait_ge(sm_step, n * 5 + 10)
                    for mt in range(2):
                        for t in range(TT):
                            ins = pe.transpose(S[:, mt * T + t * P:mt * T + (t + 1) * P],
                                               prob[:, t, mt * P:(mt + 1) * P], ident[:])
                    ins.then_inc(pt_done, 1)
                    gemm(6, xs)
                    got(5)
                    v_turn(0, v_f, VO)
                    tri(0)
                    y_part(0)
                    y_part(1)
                    gemm(7, xs)
                    attend(0)
                    gemm(8, xs)
                    got(7)
                    z(1)
                    y_part(2)
                    gemm(9, mT)
                    tri(1)
                    got(8)
                    pe.wait_ge(o_lo, n * 3 + 2)
                    v_turn(1, v_f, VO)
                    y_part(3)
                    got(9)
                    pe.wait_ge(pt_copied, n + 2)
                    v_turn(2, vm_f, S)
                    attend(1)
                    pe.wait_ge(v_copied, n * 3 + 4)
                    for mt in range(2):
                        ins = pe.matmul(S[:, T:2 * T], vm_s[:, mt, :], probT[:, mt, :], start=mt == 0, stop=mt == 1)
                    ins.then_inc(attn_done, 1)
                pe.wait_ge(gelu_step, (4 * l + 3) * 5 + 10)
                pe.wait_ge(bu_copied, 16 * l + 18)
                for c in range(2):
                    for h in range(2):
                        t = 2 * c + h
                        s = hl_slot("GLU", c, h)
                        pe.wait_ge(lo_ready, chunk_no("GLU", l, 0, c) * 2 + h + 1 + HALF_CREDIT)
                        for ab in range(2):
                            kk = 2 * t + ab
                            pe.wait_ge(tile_out, tile_no("GLU", l, 0, kk) + 1)
                            dst = bank[kk % 4]
                            for k in range(4):
                                w = slice(k * 256 + ab * P, k * 256 + (ab + 1) * P)
                                pe.matmul(dst[:, :], hi[:, s, w], gT[:, k, :], start=k == 0, stop=False)
                                ins = pe.matmul(dst[:, 0:T], lo[:, s, w], gT[:, k, 0:T], start=False, stop=k == 3)
                        ins.then_inc(half_done, 1)
                pe.wait_ge(w_ready, 8 * (l + 1) + 1)
                pe.wait_ge(pt_copied, 4 * (l + 1) + 1)
                pe.wait_ge(o_lo, 12 * (l + 1) + 1)
                with pe.Fori(0, 16) as i:
                    def gate_product(c, k):
                        pe.wait_ge(tile_out, tile_no("G", l, i, k) - 1)
                        for h in range(2):
                            product("G", l, i, c, h, bank[k], xs, 8 * h, h == 0, h == 1)

                    gate_product(0, 0)
                    pe.wait_ge(tile_out, tile_no("G", l, i, 1) - 1)
                    product("G", l, i, 1, 0, bank[1], sbT, 0, True, True)
                    pe.wait_ge(glu_lo, 4 * l + 4)
                    pe.wait_ge(lo_ready, chunk_no("G", l, i, 1) * 2 + (2 + HALF_CREDIT))
                    s = hl_slot("G", 1, 1)
                    for b, src in ((1, ssmT), (2, mmT)):
                        pe.wait_ge(tile_out, tile_no("G", l, i, 1 + b) - 1)
                        for k in range(4):
                            w = slice((4 * (b - 1) + k) * P, (4 * (b - 1) + k + 1) * P)
                            pe.matmul(bank[1 + b][:, :], hi[:, s, w], src[:, k, :], start=k == 0, stop=False)
                            ins = pe.matmul(bank[1 + b][:, 0:T], lo[:, s, w], src[:, k, 0:T], start=False, stop=k == 3)
                    ins.then_inc(half_done, 1)
                    gate_product(2, 4)
                    gate_product(3, 5)
                pe.wait_ge(tile_out, tile_no("G", l, 15, 5) + 1 + TILE_CREDIT)
                pe.wait_ge(merge_lo, 16 * l + 17)
                with pe.Fori(0, 2) as i:
                    for nn in range(2):
                        for m in range(TT):
                            pe.wait_ge(rows_out, rows_no("WO", l, i, nn, m) + 1)
                        banks = [bank[6 - 2 * nn + m] for m in range(TT)]
                        for c in range(4):
                            for h in range(2):
                                rows_product("WO", l, i, 4 * nn + c, h, 4 * c + 2 * h, banks, c == 0 and h == 0,
                                             c == 3 and h == 1)
                norm(l, 0)
                pe.wait_ge(resid_act, 4 * (2 * l) + 2)
                pe.wait_ge(resid_dve, 4 * (2 * l) + 2)
                with pe.Fori(0, 11) as i:
                    n = i + 11 * l
                    for c in range(8):
                        pe.wait_ge(tile_out, tile_no("FF", l, i, c) - 1)
                        for h in range(2):
                            product("FF", l, i, c, h, bank[2 * ((c // 2) % 2) + c % 2], xs, 8 * h, h == 0, h == 1)
                    pe.wait_ge(resid_act, 4 * (2 * l) + 4)
                    pe.wait_ge(resid_dve, 4 * (2 * l) + 4)
                    for nn in range(4):
                        for m in range(TT):
                            pe.wait_ge(rows_out, rows_no("FF", l, i, nn, m) + 1)
                        banks = [bank[6 - 2 * (nn % 2) + m] for m in range(TT)]
                        for h in range(2):
                            rows_product("FF", l, i, 8 + nn, h, 2 * h, banks, h == 0, h == 1,
                                         ready=(lambda k: (ffn_lo, n * 4 + (k + 3))) if nn == 0 else None)
                if l < DEPTH - 1:
                    norm(l, 1)


def hl_slot(ph, c, h):
    return (2 * c + h) % HLS


SETUP_STEPS = 138

_INS = ["x", "mem", "w_in", "b_in", "sb_w_out", "ssm_lambda_re", "ssm_lambda_im", "ssm_log_dt", "ssm_b_re",
        "ssm_b_im", "ssm_c_re", "ssm_c_im", "ssm_d", "ssm_w_glu", "ssm_w_out", "mem_w_kv", "mem_w_out", "w_o",
        "ln1_g", "ln1_b", "ffn_w_gate_up", "ffn_w_down", "ln2_g", "ln2_b"]


def kernel(**inputs):
    import concourse.bacc as bacc
    from concourse.bass_utils import run_bass_kernel_spmd

    nc = bacc.Bacc("TRN2", target_bir_lowering=False, num_devices=1, dynamic_dma_scratch_size=1024)
    arrays, args = {}, []
    for name in _INS:
        a = np.ascontiguousarray(inputs[name])
        arrays[f"in_{name}"] = a
        args.append(nc.dram_tensor(f"in_{name}", a.shape, mybir.dt.from_np(a.dtype), kind="ExternalInput").ap())
    out = nc.dram_tensor("out_x", (1, T, D), F32, kind="ExternalOutput").ap()
    trunk(nc, *args, out)
    r = run_bass_kernel_spmd(nc, [arrays], core_ids=[0])
    return r.results[0]["out_x"]
```

```python
from contextlib import ExitStack

import numpy as np

import concourse.bass as bass
from concourse import mybir

F32 = mybir.dt.float32
F32R = mybir.dt.float32r
BF16 = mybir.dt.bfloat16
I32 = mybir.dt.int32
ACT = mybir.ActivationFunctionType
ALU = mybir.AluOpType
AX_X = mybir.AxisListType.X

P = 128
T = 256
TT = T // P
D = 2048
KD = D // P
DEPTH = 2
HEADS = 8
SBW = HEADS * P
SSMW = 512
GROUPS = 32
STATE = 64
GC = 16
MEMW = 512
IN_W = 3 * SBW + SSMW + MEMW + 3 * D
D_FF = 5632
SCALE = float(P) ** -0.5
ALPHA = float((2 * DEPTH) ** 0.25)
EPS = 1e-5

CHUNK = 2048
HALF = CHUNK // 2
RAWS = 4
HLS = 4

PHASES = {
    "U": (1, [1, 2], [1, 1]),
    "BR": (3, [0, 1, 2, 3, 0, 1, 2, 3, 1, 2], [1] * 10),
    "BL": (1, [0, 1, 2, 3, 0, 1, 2, 3], [1] * 8),
    "GLU": (1, [1, 2], [4, 4]),
    "G": (16, [0, 1, 2, 3], [1, 3, 1, 1]),
    "WO": (2, [0, 1, 2, 3] * 2, [1] * 8),
    "FF": (11, [0, 1, 2, 3] * 3, [1] * 12),
}
ORDER = ["U", "BR", "BL", "GLU", "G", "WO", "FF"]
TILES = {"U": 2, "BR": 10, "BL": 8, "GLU": 8, "G": 6, "WO": 0, "FF": 8}


def _bases(per_turn):
    base, total = {}, 0
    for ph in ORDER:
        base[ph] = total
        total += PHASES[ph][0] * per_turn[ph]
    return base, total


CH_BASE, CH_LAYER = _bases({ph: len(PHASES[ph][1]) for ph in ORDER})
TILE_BASE, TILE_LAYER = _bases(TILES)
FILL_BASE = {s: _bases({ph: sum(d for q, d in zip(*PHASES[ph][1:]) if q == s) for ph in ORDER})
             for s in range(RAWS)}
CH_ALL = DEPTH * CH_LAYER


def chunk_no(ph, l, i, c):
    return i * len(PHASES[ph][1]) + (l * CH_LAYER + CH_BASE[ph] + c)


def tile_no(ph, l, i, k):
    return i * TILES[ph] + (l * TILE_LAYER + TILE_BASE[ph] + k)


def filled(ph, l, i, c):
    _, slots, dmas = PHASES[ph]
    s = slots[c]
    base, total = FILL_BASE[s]
    per = sum(d for q, d in zip(slots, dmas) if q == s)
    upto = sum(d for q, d in zip(slots[:c + 1], dmas) if q == s)
    return i * (16 * per) + 16 * (l * total + base[ph] + upto)


def reuse_distance(ph, c):
    turns, slots, _ = PHASES[ph]
    own = [c - k for k in range(c) if slots[k] == slots[c]]
    if own:
        return min(own)
    before = PHASES[ORDER[ORDER.index(ph) - 1]][1]
    wrap = [len(slots) - k + c for k in range(len(slots)) if slots[k] == slots[c] and turns > 1]
    enter = [len(before) - k + c for k in range(len(before)) if before[k] == slots[c]]
    return min(wrap + enter + [4])


HALF_CREDIT = HLS
TILE_CREDIT = 2
ROWS_CREDIT = 4

LN_STEPS = 13
GATES = ((0, 0, 0), (1, 2, 4), (2, 3, 5))
SCAN_STEPS = 10


def trunk(nc, x, mem, w_in, b_in, sb_w_out, lam_re_d, lam_im_d, log_dt_d, b_re_d, b_im_d, c_re_d,
          c_im_d, ssm_d, w_glu, ssm_w_out, w_kv, mem_w_out, w_o, ln1_g, ln1_b, w_gu, w_down,
          ln2_g, ln2_b, out):
    ctx = ExitStack()
    with ctx:
        def sb(name, shape, dt=F32, stack=ctx):
            return stack.enter_context(nc.sbuf_tensor(name, shape, dt))

        def sem(name):
            return ctx.enter_context(nc.semaphore(name))

        memT_save = nc.dram_tensor("memT_save", (P, KD * 2 * T), F32, kind="Internal").ap()
        tab_save = nc.dram_tensor("tab_save", (DEPTH * 4, P, 4 * P), F32, kind="Internal").ap()

        raw = sb("raw", [P, RAWS, CHUNK])
        hi = sb("hi", [P, HLS, HALF], F32R)
        lo = sb("lo", [P, HLS, HALF], F32R)
        xs = sb("xs", [P, KD, 2 * T], F32R)
        mT = sb("mT", [P, KD, 2 * T], F32R)
        rows = sb("rows", [P, TT, D])
        tmp = sb("tmp", [P, 2, T])

        region = ExitStack()
        sbT = sb("sbT", [P, HEADS, 2 * T], F32R, region)
        mmT = sb("mmT", [P, 4, 2 * T], F32R, region)
        gT = sb("gT", [P, 4, 2 * T], F32R, region)
        region.close()
        region = ExitStack()
        b_nat = sb("b_nat", [P, 2, 32, GC], stack=region)
        b_bar = sb("b_bar", [P, 4, 32, GC], stack=region)
        c_nat = sb("c_nat", [P, 2, 8, STATE], stack=region)
        b_blk = sb("b_blk", [P, 2, 8, P], stack=region)
        c_blk = sb("c_blk", [P, 2, 8, P], stack=region)
        region.close()
        hold_a = sb("hold_a", [P, 16 * 2 * T])

        region = ExitStack()
        scan = sb("scan", [P, 4, 2, T], stack=region)
        blocks = sb("blocks", [P, 2, 2, 2, 32 + T // 4], stack=region)
        scan_t = sb("scan_t", [P, 2, 2, T // 2], stack=region)
        region.close()
        region = ExitStack()
        ssmT = sb("ssmT", [P, 4, 2 * T], F32R, region)
        region.close()
        region = ExitStack()
        stage = sb("stage", [P, 5, 4 * P], stack=region)
        ssm_nat = sb("ssm_nat", [P, 3, P], stack=region)
        dt_nat = sb("dt_nat", [P, 2], stack=region)
        region.close()
        hold_b = sb("hold_b", [P, 3328])

        region = ExitStack()
        u_f = sb("u_f", [P, T], stack=region)
        q_f = sb("q_f", [P, T], stack=region)
        k_f = sb("k_f", [P, T], stack=region)
        v_f = sb("v_f", [P, T], stack=region)
        qm_f = sb("qm_f", [P, T], stack=region)
        km_f = sb("km_f", [P, T], stack=region)
        vm_f = sb("vm_f", [P, T], stack=region)
        v_s = sb("v_s", [P, 2, P], stack=region)
        vm_s = sb("vm_s", [P, 2, P], stack=region)
        soft = sb("soft", [P, 384], stack=region)
        sp_t = sb("sp_t", [P, 384], stack=region)
        w_t = sb("w_t", [P, 384], stack=region)
        prob = sb("prob", [P, 2, T], stack=region)
        probT = sb("probT", [P, 2, T], stack=region)
        gel_y = sb("gel_y", [P, T], stack=region)
        gel_t = sb("gel_t", [P, T], stack=region)
        region.close()
        region = ExitStack()
        mem_rows = sb("mem_rows", [P, TT, D], stack=region)
        sc = sb("sc", [P, 24, 32], stack=region)
        sci = sb("sci", [P, 3, 32], I32, region)
        region.close()
        region = ExitStack()
        gate = sb("gate", [P, 3, T], stack=region)
        bran = sb("bran", [P, 3, T], stack=region)
        acc = sb("acc", [P, T], stack=region)
        part = sb("part", [P, T], stack=region)
        region.close()
        region = ExitStack()
        gg = sb("gg", [P, 2, T], stack=region)
        th = sb("th", [P, 2, T], stack=region)
        uu = sb("uu", [P, 2, T], stack=region)
        hh = sb("hh", [P, 2, T], stack=region)
        region.close()
        region = ExitStack()
        xf = sb("xf", [P, 4, T], stack=region)
        region.close()
        hold_c = sb("hold_c", [P, 5120])

        tab = sb("tab", [P, 4, P])
        par_nat = sb("par_nat", [P, 3, P])
        par = sb("par", [P, 3, P])
        qb_s = sb("qb_s", [P, DEPTH, HEADS])
        ident = sb("ident", [P, P])
        ident_r = sb("ident_r", [P, P], F32R)
        ident_b = sb("ident_b", [P, P], BF16)
        ntri = sb("ntri", [P, P])
        nones = sb("nones", [P, P])
        causal = sb("causal", [P, P])
        nbig = sb("nbig", [P, P], BF16)
        powers = sb("powers", [P, 24, 32])
        pw = sb("pw", [P, 24, 4])
        sm = sb("sm", [P, 8])
        st = sb("st", [P, TT, 4, 6])
        mv = sb("mv", [P, TT, 2])
        rv = sb("rv", [P, 4, TT])
        odd = sb("odd", [P, 4])
        oddi = sb("oddi", [P, 1], I32)

        bank = [ctx.enter_context(nc.psum_tensor(f"bank{b}", [P, 512], F32)) for b in range(8)]
        BU, Z, S, VO, Y = (bank[2], bank[3]), bank[4], bank[5], bank[6], bank[7]

        raw_full = [sem(f"raw_full{s}") for s in range(RAWS)]
        hi_ready, lo_ready, half_done = sem("hi_ready"), sem("lo_ready"), sem("half_done")
        first_out, tile_out, rows_out = sem("first_out"), sem("tile_out"), sem("rows_out")
        odd_step, dt_step, c_out = sem("odd_step"), sem("dt_step"), sem("c_out")
        ssm_T, ssm_out, bc_in = sem("ssm_T"), sem("ssm_out"), sem("bc_in")
        x_in, mem_in, par_in, ssm_in = sem("x_in"), sem("mem_in"), sem("par_in"), sem("ssm_in")
        masks, consts = sem("masks"), sem("consts")
        par_T, par_out = sem("par_T"), sem("par_out")
        init_T, init_hi, init_lo = sem("init_T"), sem("init_hi"), sem("init_lo")
        setup = sem("setup")
        tab_T, tab_out = sem("tab_T"), sem("tab_out")
        tab_saved = [sem(f"tab_saved{q}") for q in range(5)]
        memT_saved, memT_full = sem("memT_saved"), sem("memT_full")
        tab_b_full, tab_c_full, du_done = sem("tab_b_full"), sem("tab_c_full"), sem("du_done")
        pw_ready, pads = sem("pw_ready"), sem("pads")
        bu_done, bu_copied, ks_step, y_done = sem("bu_done"), sem("bu_copied"), sem("ks_step"), sem("y_done")
        gelu_step, gelu_act = sem("gelu_step"), sem("gelu_act")
        z_done, soft_act, sp_step, tri_done, w_ready = (sem("z_done"), sem("soft_act"), sem("sp_step"),
                                                        sem("tri_done"), sem("w_ready"))
        vt_done, v_copied, attn_done = sem("vt_done"), sem("v_copied"), sem("attn_done")
        s_done, sm_step, p_exp = sem("s_done"), sem("sm_step"), sem("p_exp")
        pt_done, pt_copied, o_hi, o_lo = sem("pt_done"), sem("pt_copied"), sem("o_hi"), sem("o_lo")
        glu_th, glu_m, glu_hi, glu_lo = sem("glu_th"), sem("glu_m"), sem("glu_hi"), sem("glu_lo")
        gate_th, merge_step, merge_hi, merge_lo = (sem("gate_th"), sem("merge_step"), sem("merge_hi"),
                                                   sem("merge_lo"))
        stats_done, ln_step, norm_done, ln_T = sem("stats_done"), sem("ln_step"), sem("norm_done"), sem("ln_T")
        aff_dve, aff_act, xs_hi, xs_lo = sem("aff_dve"), sem("aff_act"), sem("xs_hi"), sem("xs_lo")
        rebuilt, resid_act, resid_dve = sem("rebuilt"), sem("resid_act"), sem("resid_dve")
        ffn_th, ffn_step, ffn_hi, ffn_lo = sem("ffn_th"), sem("ffn_step"), sem("ffn_hi"), sem("ffn_lo")
        gb_in, stored = sem("gb_in"), sem("stored")
        dve_affine, pool_affine = sem("dve_affine"), sem("pool_affine")

        def bias_col(l, tile):
            return par[:, l, bass.ds(tile, 1)]

        def norm_cols(l, which, k):
            if which == 0:
                return par[:, l, 80 + k:81 + k], par[:, l, 96 + k:97 + k]
            return par[:, 2, 32 * l + k:32 * l + k + 1], par[:, 2, 32 * l + 16 + k:32 * l + 17 + k]

        def rows_no(ph, l, i, n, m):
            return (l * 96 + (8 if ph == "FF" else 0) + 2 * n + m) + i * (8 if ph == "FF" else 4)

        def next_chunk(ph, l, i, c):
            if c + 1 < len(PHASES[ph][1]):
                return ph, l, i, c + 1
            if PHASES[ph][0] > 1:
                return ph, l, i + 1, 0
            return ORDER[ORDER.index(ph) + 1], l, 0, 0

        MAGIC = 12582912.0

        def V(k):
            return sc[:, k, :]

        def chain(eng, done, spare):
            step = [0]

            def link(ins):
                step[0] += 1
                ins.then_inc(done, 1)
                eng.wait_ge(done, step[0])

            def ts(dst, a, s1, s2=None, op0=ALU.mult, op1=None):
                link(eng.tensor_scalar(dst, a, s1, s2, op0, op1) if op1 else eng.tensor_scalar(dst, a, s1, None, op0))

            def tt(dst, a, b, op):
                link(eng.tensor_tensor(dst, a, b, op))

            def stt(dst, a, s, b, op0, op1):
                if spare == 0:
                    ts(V(21), a, s, None, op0)
                    tt(dst, V(21), b, op1)
                else:
                    link(eng.scalar_tensor_tensor(out=dst, in0=a, scalar=s, in1=b, op0=op0, op1=op1))

            def exp(dst, src, k, r):
                ts(V(r), V(src), -87.0, 88.7, ALU.max, ALU.min)
                ts(V(k), V(r), 1.4426950408889634, MAGIC, ALU.mult, ALU.add)
                ts(V(k), V(k), -MAGIC, None, ALU.add)
                stt(V(r), V(k), -0.693359375, V(r), ALU.mult, ALU.add)
                stt(V(r), V(k), 2.12194440e-4, V(r), ALU.mult, ALU.add)
                ts(V(dst), V(r), 1.0 / 5040)
                for c in (1.0 / 720, 1.0 / 120, 1.0 / 24, 1.0 / 6, 0.5, 1.0):
                    stt(V(dst), V(dst), c, V(r), ALU.add, ALU.mult)
                power = sci[:, spare, :]
                ts(power, V(k), 127.0, 8388608.0, ALU.add, ALU.mult)
                stt(V(dst), V(dst), 1.0, power.bitcast(F32), ALU.add, ALU.mult)

            return link, ts, tt, stt, exp, step

        DVE_PIECES = [(0, 0), (0, 1), (0, 2), (0, 3), (1, 3)]
        POOL_PIECES = [(1, 0), (1, 1), (1, 2)]

        def piece(t, m, c):
            return t[:, m, 512 * c:512 * c + 512]

        block = ctx.enter_context(nc.Block())

        @block.sync
        def _(sp):
            for j, d in enumerate((lam_re_d, lam_im_d)):
                sp.dma_start(ssm_nat[0:GROUPS, j, :], d.rearrange("l (j g) p -> (l j) (g p)", g=2)
                              ).then_inc(ssm_in, 16)
            sp.dma_start(dt_nat[0:GROUPS, :], log_dt_d.rearrange("l (j g) -> (l j) g", g=2)).then_inc(ssm_in, 16)
            sp.dma_start(rows[:], x.rearrange("b (m p) d -> p (b m) d", p=P)).then_inc(x_in, 16)
            sp.dma_start(mem_rows[:], mem.rearrange("b (m p) d -> p (b m) d", p=P)).then_inc(mem_in, 16)

            def load(ph, l, i, c, pieces):
                g = chunk_no(ph, l, i, c)
                if ph != "U" or l:
                    sp.wait_ge(lo_ready, g * 2 + (HALF_CREDIT + 2 - 2 * reuse_distance(ph, c)))
                slot = PHASES[ph][1][c]
                for dst, src in pieces(raw[:, slot, :]):
                    sp.dma_start(dst, src).then_inc(raw_full[slot], 16)

            def columns(w, col):
                return lambda r: [(r.rearrange("p (k n) -> p k n", n=P),
                                   w.rearrange("(k p) n -> p k n", p=P)[:, :, bass.ds(col, P)])]

            for l in range(DEPTH):
                w, w_mem = w_in[l], w_kv[l]
                load("U", l, 0, 0, columns(w_mem, MEMW))
                load("U", l, 0, 1, columns(w, 3 * SBW))

                def branch_turn(ph, i, t):
                    cols = [(w, (t + (3 * SBW + SSMW) // P) * P), (w_mem, t * P),
                            (w, t * 256), (w, t * 256 + SBW), (w, t * 256 + 2 * SBW),
                            (w, t * 256 + P), (w, t * 256 + SBW + P), (w, t * 256 + 2 * SBW + P)]
                    if ph == "BR":
                        cols += [(w_mem, (t + (MEMW // P + 1)) * P), (w, (t + (3 * SBW // P + 1)) * P)]
                    for c, (src, col) in enumerate(cols):
                        load(ph, l, i, c, columns(src, col))

                with sp.Fori(0, 3) as i:
                    branch_turn("BR", i, i)
                branch_turn("BL", 0, 3)
                for c in range(2):
                    gv = w_glu[l].rearrange("(k p) (ab t n) -> t p k ab n", p=P, ab=2, n=P)

                    def pieces(r, c=c, gv=gv):
                        rr = r.rearrange("p (t k ab n) -> p t k ab n", t=2, k=4, ab=2)
                        return [(rr[:, t, :, ab], gv[2 * c + t][:, :, ab]) for t in range(2) for ab in range(2)]
                    load("GLU", l, 0, c, pieces)
                with sp.Fori(0, 16) as i:
                    def load_gate(b, c):
                        load("G", l, i, c, columns(w_in[l], (i + (3 * SBW + SSMW + MEMW + b * D) // P) * P))

                    def pieces(r):
                        rr = r.rearrange("p (k n) -> p k n", n=P)
                        at, got = 0, []
                        for w in (sb_w_out[l], ssm_w_out[l], mem_w_out[l]):
                            v = w.rearrange("(k p) n -> p k n", p=P)
                            k = v.shape[1]
                            got.append((rr[:, at:at + k, :], v[:, :, bass.ds(i * P, P)]))
                            at += k
                        return got
                    load_gate(0, 0)
                    load("G", l, i, 1, pieces)
                    load_gate(1, 2)
                    load_gate(2, 3)

                def block_rows(w, k0, col, n=4):
                    v = w.rearrange("(k p) n -> p k n", p=P)
                    return lambda r: [(r.rearrange("p (k n) -> p k n", n=512), v[:, k0, col])]

                with sp.Fori(0, 2) as i:
                    for c in range(8):
                        load("WO", l, i, c, block_rows(w_o[l], slice(4 * (c % 4), 4 * (c % 4) + 4),
                                                       bass.ds(i * 1024 + 512 * (c // 4), 512)))
                with sp.Fori(0, 11) as i:
                    for f in range(4):
                        load("FF", l, i, 2 * f, columns(w_gu[l], i * 512 + f * P))
                        load("FF", l, i, 2 * f + 1, columns(w_gu[l], i * 512 + (D_FF + f * P)))
                    for n in range(4):
                        load("FF", l, i, 8 + n, block_rows(w_down[l], bass.ds(i * 4, 4),
                                                           slice(512 * n, 512 * n + 512)))
            sp.wait_ge(lo_ready, 2 * CH_ALL + HALF_CREDIT)
            for j, v in enumerate((ln2_g[DEPTH - 1], ln2_b[DEPTH - 1])):
                sp.dma_start(raw[:, j, :], bass.AP(tensor=v.tensor, offset=v.offset, ap=[[0, P], [1, D]])
                             ).then_inc(gb_in, 16)
            for j, (m, c) in enumerate(DVE_PIECES):
                if j < len(POOL_PIECES):
                    mp, cp = POOL_PIECES[j]
                sp.wait_ge(dve_affine, 2 * j + 2)
                sp.dma_start(out[0, m * P:(m + 1) * P, 512 * c:512 * c + 512], piece(rows, m, c)).then_inc(stored, 16)
                if j < len(POOL_PIECES):
                    sp.wait_ge(pool_affine, 3 * j + 3)
                    sp.dma_start(out[0, mp * P:(mp + 1) * P, 512 * cp:512 * cp + 512], piece(rows, mp, cp)
                                 ).then_inc(stored, 16)
            sp.wait_ge(stored, 16 * TT * 4)

        @block.gpsimd
        def _(pool):
            pool.memset(ident[:], 0.0).then_inc(masks, 1)
            pool.memset(ntri[:], -1.0).then_inc(masks, 1)
            pool.memset(nones[:], -1.0).then_inc(masks, 1)
            pool.memset(causal[:], 1.0).then_inc(masks, 1)
            pool.memset(nbig[:], -1e30).then_inc(masks, 1)
            pool.iota(oddi[:], pattern=[[0, 1]], base=0, channel_multiplier=1).then_inc(masks, 1)
            pool.wait_ge(masks, 6)
            pool.affine_select(out=ident[:], in_=ident[:], compare_op=ALU.not_equal, fill=1.0, base=0,
                               pattern=[[-1, P]], channel_multiplier=1).then_inc(masks, 1)
            pool.affine_select(out=ntri[:], in_=ntri[:], compare_op=ALU.is_ge, fill=0.0, base=0,
                               pattern=[[-1, P]], channel_multiplier=1).then_inc(masks, 1)
            pool.affine_select(out=causal[:], in_=causal[:], compare_op=ALU.is_gt, fill=0.0, base=0,
                               pattern=[[1, P]], channel_multiplier=-1).then_inc(masks, 1)
            pool.affine_select(out=nbig[:], in_=nbig[:], compare_op=ALU.is_ge, fill=0.0, base=0,
                               pattern=[[-1, P]], channel_multiplier=1).then_inc(masks, 1)

            link, ts, tt, stt, exp, count = chain(pool, setup, 0)
            pool.wait_ge(ssm_in, 48)
            link(pool.memset(b_blk[:].rearrange("p a q c -> p (a q c)"), 0.0))
            link(pool.tensor_copy(ssm_nat[0:GROUPS, 2, :].rearrange("p (g s) -> p g s", g=2),
                                  dt_nat[0:GROUPS, :].rearrange("p (g s) -> p g s", s=1)
                                  .broadcast_to([GROUPS, 2, STATE])))
            pool.wait_ge(dt_step, ANGLE_STEPS)
            tt(V(9), V(5), V(5), ALU.mult)
            ts(V(10), V(9), -1.9515295891e-4, 8.3321608736e-3, ALU.mult, ALU.add)
            tt(V(10), V(10), V(9), ALU.mult)
            stt(V(10), V(10), -1.6666654611e-1, V(9), ALU.add, ALU.mult)
            stt(V(10), V(10), 1.0, V(5), ALU.add, ALU.mult)
            ts(V(11), V(9), 2.443315711809948e-5, -1.388731625493765e-3, ALU.mult, ALU.add)
            tt(V(11), V(11), V(9), ALU.mult)
            stt(V(11), V(11), 4.166664568298827e-2, V(9), ALU.add, ALU.mult)
            stt(V(11), V(11), -0.5, V(9), ALU.add, ALU.mult)
            ts(V(11), V(11), 1.0, None, ALU.add)
            ts(V(14), V(4), 0.5, -0.25, ALU.mult, ALU.add)
            ts(V(14), V(14), MAGIC, None, ALU.add)
            ts(V(14), V(14), -MAGIC, None, ALU.add)
            stt(V(12), V(14), -2.0, V(4), ALU.mult, ALU.add)
            ts(V(13), V(14), 0.5, -0.25, ALU.mult, ALU.add)
            ts(V(13), V(13), MAGIC, None, ALU.add)
            ts(V(13), V(13), -MAGIC, None, ALU.add)
            stt(V(13), V(13), -2.0, V(14), ALU.mult, ALU.add)
            tt(V(14), V(12), V(13), ALU.subtract)
            tt(V(14), V(14), V(14), ALU.mult)
            ts(V(15), V(12), -1.0, 1.0, ALU.mult, ALU.add)
            tt(V(16), V(10), V(15), ALU.mult)
            tt(V(17), V(11), V(12), ALU.mult)
            tt(V(16), V(16), V(17), ALU.add)
            tt(V(17), V(11), V(15), ALU.mult)
            tt(V(18), V(10), V(12), ALU.mult)
            tt(V(17), V(17), V(18), ALU.add)
            pool.wait_ge(dt_step, DT_STEPS)
            for k in (13, 14):
                ts(V(k), V(k), -2.0, 1.0, ALU.mult, ALU.add)
                tt(V(k + 3), V(k + 3), V(k), ALU.mult)
                tt(V(k + 3), V(k + 3), V(8), ALU.mult)
            link(pool.tensor_copy(powers[:, 0, :], V(17)))
            link(pool.tensor_copy(powers[:, 8, :], V(16)))
            ts(V(4), powers[:, 0, :], -1.0, None, ALU.add)
            tt(V(9), V(4), V(0), ALU.mult)
            tt(V(10), powers[:, 8, :], V(1), ALU.mult)
            tt(V(9), V(9), V(10), ALU.add)
            tt(V(9), V(9), V(20), ALU.mult)
            tt(V(10), powers[:, 8, :], V(0), ALU.mult)
            tt(V(11), V(4), V(1), ALU.mult)
            tt(V(10), V(10), V(11), ALU.subtract)
            tt(V(10), V(10), V(20), ALU.mult)
            f_re = sc[:, 9:10, :].rearrange("p a j -> p j a").broadcast_to([P, 32, GC])
            f_im = sc[:, 10:11, :].rearrange("p a j -> p j a").broadcast_to([P, 32, GC])
            pool.wait_ge(bc_in, 16 * 8)
            tt(b_bar[:, 0], b_nat[:, 0], f_re, ALU.mult)
            tt(b_bar[:, 1], b_nat[:, 1], f_im, ALU.mult)
            tt(b_bar[:, 2], b_nat[:, 1], f_re, ALU.mult)
            tt(b_bar[:, 3], b_nat[:, 0], f_im, ALU.mult)
            tt(b_bar[:, 0], b_bar[:, 0], b_bar[:, 1], ALU.subtract)
            tt(b_bar[:, 2], b_bar[:, 2], b_bar[:, 3], ALU.add)
            for r in range(2):
                for g2 in range(2):
                    v = b_blk[64 * g2:64 * g2 + 64, r].rearrange("p q (j c) -> p (q j) c", c=32)
                    link(pool.tensor_copy(v[:, :, GC * g2:GC * g2 + GC], b_bar[64 * g2:64 * g2 + 64, 2 * r]))

            assert count[0] == BLOCK_STEPS, count
            for k in range(8):
                re, im = powers[:, k, :], powers[:, 8 + k, :]
                ts(powers[:, 16 + k, :], im, -1.0)
                if k < 7:
                    tt(V(4), re, re, ALU.mult)
                    tt(V(5), im, im, ALU.mult)
                    tt(powers[:, k + 1, :], V(4), V(5), ALU.subtract)
                    stt(powers[:, 9 + k, :], re, 2.0, im, ALU.mult, ALU.mult)
            pool.wait_ge(par_out, 2)
            for l in range(DEPTH):
                ts(qb_s[:, l, :], par[:, l, 0:HEADS], SCALE)
            assert count[0] == SETUP_STEPS, count
            pool.wait_ge(init_T, KD)
            pool.tensor_scalar(rows[:], rows[:], ALPHA, None, ALU.mult).then_inc(consts, 1)

            for l in range(DEPTH):
                with pool.Fori(0, 4) as turn:
                    n = turn + 4 * l
                    pool.wait_ge(sm_step, n * 5 + 8)
                    by = sm[:, 6:8].rearrange("p (a c) -> p a c", c=1).broadcast_to([P, TT, T])
                    pool.tensor_tensor(prob[:], prob[:], by, ALU.mult).then_inc(sm_step, 2)
                    for e in range(2):
                        pool.wait_ge(sp_step, n * 4 + (2 * e + 3))
                        v = sp_t[:].rearrange("p (a c) -> p a c", a=3)[:, 0:3:2, :]
                        cm = causal[:].rearrange("p (a c) -> p a c", a=1).broadcast_to([P, 2, P])
                        pool.tensor_tensor(v, v, cm, ALU.mult).then_inc(sp_step, 1)
                if l == 0:
                    pool.wait_ge(memT_saved, 16)
                with pool.Fori(0, 16) as i:
                    n = i + 16 * l
                    pool.wait_ge(merge_step, n * 5 + 10)
                    pool.tensor_copy(mT[:, bass.ds(i, 1), 0:T], acc[:]).then_inc(merge_hi, 1)
                    pool.wait_ge(merge_hi, n + 1)
                    pool.tensor_tensor(mT[:, bass.ds(i, 1), T:2 * T], acc[:], mT[:, bass.ds(i, 1), 0:T].bitcast(F32),
                                       ALU.subtract).then_inc(merge_lo, 1)

            pool.wait_ge(gb_in, 32)
            pool.wait_ge(ln_step, LN_STEPS * 2 * DEPTH)
            for j, (m, c) in enumerate(POOL_PIECES):
                y = piece(rows, m, c)
                pool.tensor_scalar(y, y, mv[:, m, 0:1], rv[:, 1, m:m + 1], ALU.subtract, ALU.mult
                                   ).then_inc(pool_affine, 1)
                pool.wait_ge(pool_affine, 3 * j + 1)
                pool.tensor_tensor(y, y, piece(raw, 0, c), ALU.mult).then_inc(pool_affine, 1)
                pool.wait_ge(pool_affine, 3 * j + 2)
                pool.tensor_tensor(y, y, piece(raw, 1, c), ALU.add).then_inc(pool_affine, 1)

        @block.scalar
        def _(act):
            def hi_half(ph, l, i, c, h):
                slot = PHASES[ph][1][c]
                gh = chunk_no(ph, l, i, c) * 2 + h
                if h == 0:
                    act.wait_ge(raw_full[slot], filled(ph, l, i, c))
                act.wait_ge(half_done, gh + 1)
                act.activation(hi[:, hl_slot(ph, c, h), :],
                               raw[:, slot, h * HALF:(h + 1) * HALF], ACT.Copy).then_inc(hi_ready, 1)

            def split_next(ph, l, i, c):
                nxt = next_chunk(ph, l, i, c)
                for h in range(2):
                    if nxt[3] == 0:
                        slot = PHASES[nxt[0]][1][0]
                        gh = chunk_no(ph, l, i, c) * 2 + 2 + h
                        if h == 0:
                            act.wait_ge(raw_full[slot], filled(*nxt))
                        act.wait_ge(half_done, gh + 1)
                        act.activation(hi[:, hl_slot(ph, c + 1, h), :], raw[:, slot, h * HALF:(h + 1) * HALF],
                                       ACT.Copy).then_inc(hi_ready, 1)
                    else:
                        hi_half(ph, l, i, c + 1, h)

            def first_half(ph, l, i, k, src, ready, bias=None, scale=1.0):
                t = tile_no(ph, l, i, k)
                act.wait_ge(half_done, ready)
                act.wait_ge(tile_out, t + 1)
                if bias is None:
                    ins = act.activation(tmp[:, k % 2, :], src[:, 0:T], ACT.Copy, scale=scale)
                else:
                    ins = act.activation(tmp[:, k % 2, :], src[:, 0:T], ACT.Identity, bias=bias, scale=scale)
                ins.then_inc(first_out, 1)

            def done(ph, l, i, c, h=1):
                return chunk_no(ph, l, i, c) * 2 + (h + 1 + HALF_CREDIT)

            for l in range(DEPTH):
                for src, at, n in ((b_in[l], 0, 80), (ln1_g[l], 80, 16), (ln1_b[l], 96, 16),
                                   (ssm_d[l], 112, 4)):
                    act.dma_start(par_nat[at:at + n, l, :], src.rearrange("(n c) -> n c", c=P)).then_inc(par_in, 16)
                for src, at in ((ln2_g[l], 0), (ln2_b[l], 16)):
                    act.dma_start(par_nat[32 * l + at:32 * l + at + 16, 2, :],
                                 src.rearrange("(n c) -> n c", c=P)).then_inc(par_in, 16)
            def load_ssm(l):
                for j, d in enumerate((b_re_d, b_im_d)):
                    act.dma_start(b_nat[:, j, 16 * l:16 * l + 16, :],
                                  d[l].rearrange("(j g) p c -> (g p) j c", g=2)).then_inc(bc_in, 16)
                for j, d in enumerate((c_re_d, c_im_d)):
                    act.dma_start(c_nat[:, j, 4 * l:4 * l + 4, :],
                                  d[l].rearrange("(q g) c p -> (g c) q p", g=8)).then_inc(bc_in, 16)

            act.wait_ge(ssm_T, 1)
            act.activation(sc[:, 0:3, :], bank[1][:, 0:96].rearrange("p (a c) -> p a c", a=3), ACT.Copy
                           ).then_inc(ssm_out, 1)
            act.wait_ge(x_in, 16)
            load_ssm(0)
            load_ssm(1)
            for k in range(2 * KD):
                dst = xs if k < KD else mT
                act.wait_ge(init_T, k + 1)
                act.activation(dst[:, k % KD, 0:T], bank[4 + k % 4][:, 0:T], ACT.Copy).then_inc(init_hi, 1)
                if k == KD:
                    for h in range(2):
                        hi_half("U", 0, 0, 0, h)
            act.wait_ge(par_T, 1)
            act.activation(par[:, 0:2, 0:116], bank[0][:, 0:2 * P].rearrange("p (a c) -> p a c", a=2)[:, :, 0:116],
                           ACT.Copy).then_inc(par_out, 1)
            act.activation(par[:, 2, 0:64], bank[0][:, 2 * P:2 * P + 64], ACT.Copy).then_inc(par_out, 1)
            act.wait_ge(init_lo, 2 * KD)
            act.dma_start(memT_save, mT[:].rearrange("p k t -> p (k t)").bitcast(F32)).then_inc(memT_saved, 16)
            act.wait_ge(odd_step, 4)
            act.wait_ge(bc_in, 16 * 8)
            for r in range(2):
                for g2 in range(2):
                    which = 2 * r + (1 - g2)
                    act.activation(c_blk[:, r, :, 64 * g2:64 * g2 + 64], c_nat[:, r], ACT.Identity, bias=0.0,
                                   scale=odd[:, which:which + 1]).then_inc(c_out, 1)

            def load_tables(n, a, full):
                act.dma_start(tab[:, 2 * a:2 * a + 2].rearrange("p a c -> p (a c)"),
                              tab_save.rearrange("q p c -> p q c")[:, bass.ds(n, 1), 2 * a * P:(2 * a + 2) * P]
                              ).then_inc(full, 16)

            def norm(l, which):
                v = 2 * l + which
                for k in range(KD):
                    g, b = norm_cols(l, which, k)
                    if k % 2:
                        act.wait_ge(ln_T, 16 * v + k + 1)
                        if k >= 4:
                            act.wait_ge(xs_lo, 16 * v + k - 3)
                        act.activation(xf[:, k % 4, :], bank[4 + k % 4][:, 0:T], ACT.Identity, bias=b, scale=g
                                       ).then_inc(aff_act, 1)
                        act.wait_ge(aff_act, 8 * v + k // 2 + 1)
                    else:
                        act.wait_ge(aff_dve, 8 * v + k // 2 + 1)
                    act.activation(xs[:, k, 0:T], xf[:, k % 4, :], ACT.Copy).then_inc(xs_hi, 1)
                for n in range(4):
                    act.wait_ge(rebuilt, 8 * v + 2 * n + 1)
                    act.activation(rows[:, 0, 512 * n:512 * n + 512], bank[2 * n][:, :], ACT.Copy, scale=ALPHA
                                   ).then_inc(resid_act, 1)

            for l in range(DEPTH):
                for c, col in ((0, None), (1, bias_col(l, 24))):
                    split_next("U", l, 0, c)
                    first_half("U", l, 0, c, bank[c], done("U", l, 0, c), col)

                if l == 0:
                    for q in range(8):
                        act.wait_ge(tab_T, q + 1)
                        if q >= 5:
                            act.wait_ge(tab_saved[q - 5], 16)
                        act.activation(stage[:, q % 5, :], bank[2 + q % 2][:, :], ACT.Copy).then_inc(tab_out, 1)
                        act.wait_ge(tab_out, q + 1)
                        act.dma_start(tab_save[q], stage[:, q % 5, :]).then_inc(tab_saved[q % 5], 16)
                        if q == 3:
                            act.wait_ge(tab_saved[0], 16)
                            load_tables(0, 0, tab_b_full)
                    for q in range(5):
                        act.wait_ge(tab_saved[q], 32 if q < 3 else 16)
                    act.wait_ge(setup, SETUP_STEPS)
                def branch_turn(ph, i, turn):
                    n = turn + 4 * l
                    last = ph == "BL"

                    def split(c):
                        split_next(ph, l, i, c)

                    def tile(c, bias_tile=None, scale=1.0, bias=None):
                        if bias is None and bias_tile is not None:
                            bias = bias_col(l, bias_tile)
                        first_half(ph, l, i, c, bank[c % 2], done(ph, l, i, c), bias, scale)

                    def copy_bu(j):
                        act.wait_ge(bu_done, n * 4 + (j + 1))
                        act.wait_ge(y_done, n * 4 + (j + 1))
                        act.activation(scan[:, j],
                                       BU[j % 2][:, :].rearrange("p (r t) -> p r t", r=2), ACT.Copy
                                       ).then_inc(bu_copied, 1)

                    def softplus(e):
                        act.wait_ge(z_done, n * 2 + (e + 2))
                        act.wait_ge(sp_step, n * 4 + (2 * e + 1))
                        act.activation(soft[:], Z[:, 0:384], ACT.Abs).then_inc(soft_act, 1)
                        act.wait_ge(soft_act, n * 6 + (3 * e + 1))
                        act.activation(soft[:], soft[:], ACT.Exp, scale=-1.0).then_inc(soft_act, 1)
                        act.wait_ge(soft_act, n * 6 + (3 * e + 2))
                        act.activation(soft[:], soft[:], ACT.Ln, bias=1.0).then_inc(soft_act, 1)

                    def weights(e):
                        act.wait_ge(tri_done, n * 2 + (e + 2))
                        act.wait_ge(attn_done, n * 3 + (3 + e))
                        act.activation(w_t[:], Z[:, 0:384], ACT.Exp).then_inc(w_ready, 1)

                    def copy_v(k, src, dst, freed):
                        act.wait_ge(vt_done, n * 3 + (k + 4))
                        act.wait_ge(attn_done, n * 3 + freed)
                        act.activation(dst[:].rearrange("p a c -> p (a c)"), src[:, 0:T], ACT.Copy
                                       ).then_inc(v_copied, 1)

                    def out_hi(k, src, dst):
                        act.wait_ge(attn_done, n * 3 + (k + 4))
                        act.activation(dst, src[:, T:2 * T], ACT.Copy).then_inc(o_hi, 1)

                    split(0)
                    act.wait_ge(y_done, n * 4 + 4)
                    load_tables(n, 1, tab_c_full)
                    copy_bu(0)
                    copy_bu(1)
                    tile(0, turn + 28)
                    split(1)
                    copy_bu(2)
                    copy_bu(3)
                    act.wait_ge(gelu_step, n * 5 + 4)
                    act.activation(gel_y[:], u_f[:], ACT.Identity, bias=0.0, scale=bias_col(l, turn + 112)
                                   ).then_inc(du_done, 1)
                    tile(1)
                    split(2)
                    if not (last and l == DEPTH - 1):
                        act.wait_ge(bu_done, n * 4 + 4)
                        load_tables(n + 1, 0, tab_b_full)
                    tile(2, scale=SCALE, bias=qb_s[:, l, bass.ds(turn * 2, 1)])
                    split(3)
                    for t in range(TT):
                        act.wait_ge(sm_step, n * 5 + 7)
                        act.wait_ge(pt_done, n + 1)
                        act.activation(prob[:, t, :], S[:, t * T:(t + 1) * T], ACT.Exp, bias=sm[:, 2 + t:3 + t],
                                       scale=SCALE, accum_out=sm[:, 4 + t:5 + t]).then_inc(p_exp, 1)
                    tile(3, turn * 2 + 8)
                    split(4)
                    tile(4, turn * 2 + 16)
                    split(5)
                    softplus(0)
                    act.wait_ge(pt_done, n + 2)
                    act.wait_ge(attn_done, n * 3 + 2)
                    act.activation(probT[:].rearrange("p a c -> p (a c)"), S[:, :], ACT.Copy).then_inc(pt_copied, 1)
                    tile(5, scale=SCALE, bias=qb_s[:, l, bass.ds(turn * 2 + 1, 1)])
                    split(6)
                    weights(0)
                    copy_v(0, VO, v_s, 3)
                    tile(6, turn * 2 + 9)
                    split(7)
                    out_hi(0, VO, sbT[:, bass.ds(turn * 2, 1), 0:T])
                    copy_v(1, S, vm_s, 2)
                    tile(7, turn * 2 + 17)
                    if not last:
                        split(8)
                    out_hi(1, S, mmT[:, bass.ds(turn, 1), 0:T])
                    softplus(1)
                    if not last:
                        tile(8)
                        split(9)
                    weights(1)
                    copy_v(2, VO, v_s, 4)
                    act.wait_ge(gelu_step, n * 5 + 8)
                    act.activation(gel_t[:], gel_t[:], ACT.Tanh, scale=0.7978845608028654).then_inc(gelu_act, 1)
                    act.wait_ge(gelu_step, n * 5 + 9)
                    act.activation(gT[:, bass.ds(turn, 1), 0:T], gel_t[:], ACT.Copy, scale=0.5).then_inc(gelu_act, 1)
                    if not last:
                        tile(9, turn + 25)
                    out_hi(2, VO, sbT[:, bass.ds(turn * 2 + 1, 1), 0:T])

                with act.Fori(0, 3) as i:
                    branch_turn("BR", i, i)
                branch_turn("BL", 0, 3)
                for c in range(2):
                    split_next("GLU", l, 0, c)
                    for h in range(2):
                        t = 2 * c + h
                        for k in (2 * t, 2 * t + 1):
                            first_half("GLU", l, 0, k, bank[k % 4], done("GLU", l, 0, c, h))
                        act.wait_ge(tile_out, tile_no("GLU", l, 0, 2 * t + 1) + 1 + TILE_CREDIT)
                        act.activation(gate[:, 1, :], gate[:, 1, :], ACT.Tanh, scale=0.5).then_inc(glu_th, 1)
                        act.wait_ge(glu_m, 4 * l + t + 1)
                        act.activation(ssmT[:, t, 0:T], acc[:], ACT.Copy, scale=0.5).then_inc(glu_hi, 1)
                with act.Fori(0, 16) as i:
                    n = i + 16 * l
                    for b, c, k in GATES:
                        split_next("G", l, i, c)
                        first_half("G", l, i, k, bank[k], done("G", l, i, c), bias_col(l, i + (32 + 16 * b)))
                        act.wait_ge(tile_out, tile_no("G", l, i, k) + (1 + TILE_CREDIT))
                        act.activation(gate[:, b, :], gate[:, b, :], ACT.Tanh, scale=0.5).then_inc(gate_th, 1)
                        if b == 0:
                            split_next("G", l, i, 1)
                            for k in range(3):
                                first_half("G", l, i, 1 + k, bank[1 + k], done("G", l, i, 1, 0 if k == 0 else 1),
                                           scale=0.5)
                with act.Fori(0, 2) as i:
                    for c in range(8):
                        split_next("WO", l, i, c)
                norm(l, 0)
                last_l = l == DEPTH - 1

                def ffn_turn(i, last):
                    n = i + 11 * l
                    for c in range(12):
                        if not (last and last_l and c == 11):
                            split_next("FF", l, i, c) if not (last and c == 11) else split_into_next_layer()
                        if c < 8:
                            f = c // 2
                            first_half("FF", l, i, c, bank[2 * (f % 2) + c % 2], done("FF", l, i, c))
                            if c % 2:
                                act.wait_ge(tile_out, tile_no("FF", l, i, c - 1) + (1 + TILE_CREDIT))
                                act.activation(th[:, f % 2, :], gg[:, f % 2, :], ACT.Tanh, scale=0.5
                                               ).then_inc(ffn_th, 1)
                                act.wait_ge(ffn_step, n * 8 + (2 * f + 2 + 4))
                                act.activation(mT[:, f, 0:T], hh[:, f % 2, :], ACT.Copy).then_inc(ffn_hi, 1)

                def split_into_next_layer():
                    for h in range(2):
                        hi_half("U", l + 1, 0, 0, h)

                with act.Fori(0, 10) as i:
                    ffn_turn(i, False)
                ffn_turn(10, True)
                if not last_l:
                    act.wait_ge(half_done, done("FF", l, 10, 11))
                    act.dma_start(mT[:].rearrange("p k t -> p (k t)").bitcast(F32), memT_save).then_inc(memT_full, 16)
                    norm(l, 1)

        @block.vector
        def _(dve):
            dve.sem_inc(half_done, HALF_CREDIT)
            dve.sem_inc(lo_ready, HALF_CREDIT)
            dve.sem_inc(tile_out, TILE_CREDIT)
            dve.sem_inc(rows_out, ROWS_CREDIT)
            for s, v in ((y_done, 4), (bu_copied, 2), (ks_step, 1), (gelu_step, 5), (sp_step, 2), (tri_done, 1),
                         (attn_done, 3), (w_ready, 1), (v_copied, 1), (vt_done, 3), (z_done, 1), (s_done, 1),
                         (pt_copied, 1), (sm_step, 5), (pt_done, 1), (o_lo, 1), (merge_step, 5), (merge_lo, 1),
                         (ffn_step, 4), (ffn_lo, 2)):
                dve.sem_inc(s, v)
            dve.wait_ge(masks, 10)
            dve.tensor_copy(ident_r[:], ident[:]).then_inc(consts, 1)
            dve.tensor_copy(ident_b[:], ident[:]).then_inc(consts, 1)

            dve.tensor_scalar(oddi[:], oddi[:], 4, 1, ALU.logical_shift_right, ALU.bitwise_and).then_inc(odd_step, 1)
            dve.wait_ge(odd_step, 1)
            dve.tensor_copy(odd[:, 0:1], oddi[:]).then_inc(odd_step, 1)
            dve.wait_ge(odd_step, 2)
            dve.tensor_scalar(odd[:, 1:2], odd[:, 0:1], -1.0, 1.0, ALU.mult, ALU.add).then_inc(odd_step, 1)
            dve.wait_ge(odd_step, 3)
            dve.tensor_scalar(odd[:, 2:4], odd[:, 0:2], -1.0, None, ALU.mult).then_inc(odd_step, 1)

            def lo_half(slot, s, h, gh):
                dve.wait_ge(hi_ready, gh + 1)
                dve.tensor_tensor(lo[:, s, :], raw[:, slot, h * HALF:(h + 1) * HALF], hi[:, s, :].bitcast(F32),
                                  ALU.subtract).then_inc(lo_ready, 1)

            def split_next(ph, l, i, c):
                nxt = next_chunk(ph, l, i, c)
                slot = PHASES[nxt[0]][1][nxt[3]]
                for h in range(2):
                    lo_half(slot, hl_slot(ph, c + 1, h), h, chunk_no(ph, l, i, c) * 2 + (2 + h))

            def take(ph, l, i, k, src, dst, scale=1.0):
                t = tile_no(ph, l, i, k)
                dve.wait_ge(first_out, t + 1)
                dve.scalar_tensor_tensor(out=dst, in0=src[:, T:2 * T], scalar=scale, in1=tmp[:, k % 2, :],
                                         op0=ALU.mult, op1=ALU.add).then_inc(tile_out, 1)

            link, ts, tt, stt, exp, count = chain(dve, dt_step, 1)
            dve.wait_ge(ssm_out, 1)
            exp(3, 2, 22, 23)
            tt(V(6), V(0), V(3), ALU.mult)
            tt(V(7), V(1), V(3), ALU.mult)
            tt(V(18), V(0), V(0), ALU.mult)
            tt(V(19), V(1), V(1), ALU.mult)
            tt(V(19), V(18), V(19), ALU.add)
            ts(V(4), V(7), 0.6366197723675814, MAGIC, ALU.mult, ALU.add)
            ts(V(4), V(4), -MAGIC, None, ALU.add)
            stt(V(5), V(4), -1.5703125, V(7), ALU.mult, ALU.add)
            stt(V(5), V(4), -4.837512969970703125e-4, V(5), ALU.mult, ALU.add)
            stt(V(5), V(4), -7.54978995489188216e-8, V(5), ALU.mult, ALU.add)
            link(dve.reciprocal(V(20), V(19)))
            assert count[0] == ANGLE_STEPS, count

            for k in range(2 * KD):
                dst = xs if k < KD else mT
                dve.wait_ge(init_hi, k + 1)
                dve.tensor_tensor(dst[:, k % KD, T:2 * T], bank[4 + k % 4][:, 0:T],
                                  dst[:, k % KD, 0:T].bitcast(F32), ALU.subtract).then_inc(init_lo, 1)
                if k == KD - 1:
                    exp(8, 6, 22, 23)
                    assert count[0] == DT_STEPS, count
                if k == KD:
                    for h in range(2):
                        lo_half(PHASES["U"][1][0], h, h, h)

            def norm(l, which):
                v = 2 * l + which
                base = LN_STEPS * v
                k = [0]

                def lnk(ins):
                    k[0] += 1
                    ins.then_inc(ln_step, 1)
                    dve.wait_ge(ln_step, base + k[0])

                dve.wait_ge(stats_done, 8 * v + 8)
                for m in range(TT):
                    lnk(dve.bn_aggr(mv[:, m, :], st[:, m, :, :].rearrange("p a b -> p (a b)")))
                var, r, t, u = rv[:, 0, :], rv[:, 1, :], rv[:, 2, :], rv[:, 3, :]
                lnk(dve.tensor_scalar(var, mv[:, :, 1], EPS, None, ALU.add))
                lnk(dve.tensor_scalar(r.bitcast(I32), var.bitcast(I32), -0.5, float(0x5f3759df), ALU.mult, ALU.add))
                for _ in range(3):
                    lnk(dve.scalar_tensor_tensor(out=t, in0=r, scalar=-0.5, in1=r, op0=ALU.mult, op1=ALU.mult))
                    lnk(dve.tensor_tensor(u, t, var, ALU.mult))
                    lnk(dve.scalar_tensor_tensor(out=r, in0=u, scalar=1.5, in1=r, op0=ALU.add, op1=ALU.mult))
                assert k[0] == LN_STEPS
                if v == 2 * DEPTH - 1:
                    dve.wait_ge(gb_in, 32)
                    for j, (m, c) in enumerate(DVE_PIECES):
                        y = piece(rows, m, c)
                        dve.scalar_tensor_tensor(out=y, in0=y, scalar=mv[:, m, 0:1], in1=piece(raw, 0, c),
                                                 op0=ALU.subtract, op1=ALU.mult).then_inc(dve_affine, 1)
                        dve.wait_ge(dve_affine, 2 * j + 1)
                        dve.scalar_tensor_tensor(out=y, in0=y, scalar=rv[:, 1, m:m + 1], in1=piece(raw, 1, c),
                                                 op0=ALU.mult, op1=ALU.add).then_inc(dve_affine, 1)
                    return
                for c in range(4):
                    for m in range(TT):
                        y = rows[:, m, 512 * c:512 * c + 512]
                        dve.tensor_scalar(y, y, mv[:, m, 0:1], rv[:, 1, m:m + 1], ALU.subtract, ALU.mult
                                          ).then_inc(norm_done, 1)

                def affine(k):
                    g, b = norm_cols(l, which, k)
                    dve.wait_ge(ln_T, 16 * v + k + 1)
                    if k >= 4:
                        dve.wait_ge(xs_lo, 16 * v + k - 3)
                    dve.tensor_scalar(xf[:, k % 4, :], bank[4 + k % 4][:, 0:T], g, b, ALU.mult, ALU.add
                                      ).then_inc(aff_dve, 1)

                def lo_part(k):
                    dve.wait_ge(xs_hi, 16 * v + k + 1)
                    dve.tensor_tensor(xs[:, k, T:2 * T], xf[:, k % 4, :], xs[:, k, 0:T].bitcast(F32), ALU.subtract
                                      ).then_inc(xs_lo, 1)

                affine(0)
                for k in range(2, KD, 2):
                    affine(k)
                    lo_part(k - 2)
                    lo_part(k - 1)
                lo_part(KD - 2)
                lo_part(KD - 1)
                for nn in range(4):
                    dve.wait_ge(rebuilt, 8 * v + 2 * nn + 2)
                    dve.tensor_scalar(rows[:, 1, 512 * nn:512 * nn + 512], bank[2 * nn + 1][:, :], ALPHA, None,
                                      ALU.mult).then_inc(resid_dve, 1)

            def add_rows(ph, l, i, n, m, src, stats=None, ready=0, dyn=None):
                y = rows[:, m, 512 * n:512 * n + 512] if dyn is None else rows[:, m, bass.ds(dyn, 512)]
                dve.wait_ge(half_done, ready)
                dve.tensor_tensor(y, y, src[:, :], ALU.add).then_inc(rows_out, 1)
                if stats is not None:
                    dve.wait_ge(rows_out, rows_no(ph, l, i, n % 2 if ph == "WO" else n, m) + (1 + ROWS_CREDIT))
                    dve.bn_stats(stats, y).then_inc(stats_done, 1)

            for l in range(DEPTH):
                split_next("U", l, 0, 0)
                if l:
                    dve.wait_ge(vt_done, 12 * l + 3)
                take("U", l, 0, 0, bank[0], vm_f[:])
                split_next("U", l, 0, 1)
                if l:
                    dve.wait_ge(bu_done, 16 * l)
                    dve.wait_ge(du_done, 4 * l)
                take("U", l, 0, 1, bank[1], u_f[:])

                if l == 0:
                    for q in range(5):
                        dve.wait_ge(tab_saved[q], 32 if q < 3 else 16)
                dve.memset(blocks[:].rearrange("p j a r t -> p (j a r) t")[:, :, 0:32], 0.0).then_inc(pads, 1)
                dve.wait_ge(pads, l + 1)
                if l == 0:
                    dve.wait_ge(setup, SETUP_STEPS)
                def branch_turn(ph, i, turn):
                    n = turn + 4 * l
                    last = ph == "BL"

                    def split(c):
                        split_next(ph, l, i, c)

                    def tile(c, dst, scale=1.0):
                        take(ph, l, i, c, bank[c % 2], dst[:], scale)

                    def scan_states(pair, first, last_):
                        def steps(e):
                            X = scan[:, 2 * pair + e]

                            def at_times(start, stride, count):
                                return X[:, :, start:start + stride * (count - 1) + 1:stride]

                            def sums(which, back):
                                return blocks[:, e, which, :, 32 - back:32 + T // 4 - back]

                            got = [(0, at_times(0, 2, 128), at_times(1, 2, 128), at_times(1, 2, 128)),
                                   (1, at_times(1, 4, 64), at_times(3, 4, 64), sums(0, 0))]
                            for q in range(6):
                                got.append((2 + q, sums(q % 2, 1 << q), sums(q % 2, 0),
                                            sums(1 - q % 2, 0) if q < 5 else at_times(3, 4, 64)))
                            got += [(1, at_times(3, 4, 63), at_times(5, 4, 63), at_times(5, 4, 63)),
                                    (0, at_times(1, 2, 127), at_times(2, 2, 127), at_times(2, 2, 127))]
                            assert len(got) == SCAN_STEPS
                            return got

                        if first == 0:
                            dve.wait_ge(bu_copied, n * 4 + (2 * pair + 4))
                        for q in range(first, last_):
                            at = n * (12 * SCAN_STEPS) + (6 * (SCAN_STEPS * pair + q) + 1)
                            for e in range(2):
                                lev, early, late, dst = steps(e)[q]
                                dve.wait_ge(ks_step, at - 2 if e == 0 and q else at)
                                dve.scalar_tensor_tensor(out=scan_t[:, e, :, 0:early.shape[2]], in0=early,
                                                         scalar=pw[:, lev, 2 * pair + e:2 * pair + e + 1], in1=late,
                                                         op0=ALU.mult, op1=ALU.add).then_inc(ks_step, 1)
                            for e in range(2):
                                lev, early, late, dst = steps(e)[q]
                                dve.wait_ge(ks_step, at + 1 + e)
                                for r in range(2):
                                    a = pw[:, (16, 8)[r] + lev, 2 * pair + e:2 * pair + e + 1]
                                    dve.scalar_tensor_tensor(out=dst[:, r], in0=early[:, 1 - r], scalar=a,
                                                             in1=scan_t[:, e, r, 0:early.shape[2]], op0=ALU.mult,
                                                             op1=ALU.add).then_inc(ks_step, 1)

                    def softplus(e):
                        dve.wait_ge(soft_act, n * 6 + (3 * e + 3))
                        dve.wait_ge(tri_done, n * 2 + (e + 1))
                        dve.scalar_tensor_tensor(out=sp_t[:], in0=Z[:, 0:384], scalar=0.0, in1=soft[:],
                                                 op0=ALU.max, op1=ALU.add).then_inc(sp_step, 1)

                    def out_lo(k, src, dst, hi_part):
                        dve.wait_ge(o_hi, n * 3 + (k + 1))
                        dve.tensor_tensor(dst, src[:, T:2 * T], hi_part.bitcast(F32), ALU.subtract).then_inc(o_lo, 1)

                    def part_of(t, k, lo_side):
                        return t[:, bass.ds(k, 1), T:2 * T] if lo_side else t[:, bass.ds(k, 1), 0:T]

                    dve.wait_ge(ks_step, n * (12 * SCAN_STEPS) + 1)
                    dve.tensor_copy(pw[:], powers[:, :, bass.ds(n * 4, 4)]).then_inc(pw_ready, 1)
                    split(0)
                    dve.wait_ge(pw_ready, n + 1)
                    scan_states(0, 0, 2)
                    dve.wait_ge(s_done, n + 1)
                    tile(0, qm_f)
                    split(1)
                    scan_states(0, 2, 4)
                    tile(1, km_f)
                    split(2)
                    scan_states(0, 4, 6)
                    dve.wait_ge(z_done, n * 2 + 1)
                    tile(2, q_f, SCALE)
                    split(3)
                    dve.wait_ge(s_done, n + 2)
                    dve.wait_ge(sm_step, n * 5 + 5)
                    dve.tensor_reduce(sm[:, 0:2], S[:, :].rearrange("p (a c) -> p a c", a=2), AX_X, ALU.max
                                      ).then_inc(sm_step, 1)
                    dve.wait_ge(sm_step, n * 5 + 6)
                    dve.tensor_scalar(sm[:, 2:4], sm[:, 0:2], -SCALE, None, ALU.mult).then_inc(sm_step, 1)
                    scan_states(0, 6, 8)
                    tile(3, k_f)
                    split(4)
                    dve.wait_ge(p_exp, n * 2 + 2)
                    dve.reciprocal(sm[:, 6:8], sm[:, 4:6]).then_inc(sm_step, 1)
                    scan_states(0, 8, 10)
                    dve.wait_ge(vt_done, n * 3 + 3)
                    tile(4, v_f)
                    split(5)
                    scan_states(1, 0, 2)
                    softplus(0)
                    dve.wait_ge(z_done, n * 2 + 2)
                    tile(5, q_f, SCALE)
                    split(6)
                    scan_states(1, 2, 5)
                    tile(6, k_f)
                    split(7)
                    scan_states(1, 5, 7)
                    out_lo(0, VO, part_of(sbT, turn * 2, 1), part_of(sbT, turn * 2, 0))
                    dve.wait_ge(vt_done, n * 3 + 4)
                    tile(7, v_f)
                    if not last:
                        split(8)
                    scan_states(1, 7, 10)
                    out_lo(1, S, part_of(mmT, turn, 1), part_of(mmT, turn, 0))
                    softplus(1)
                    if not last:
                        dve.wait_ge(vt_done, n * 3 + 5)
                        tile(8, vm_f)
                        split(9)
                    dve.wait_ge(y_done, n * 4 + 8)
                    dve.wait_ge(du_done, n + 1)
                    dve.wait_ge(gelu_step, n * 5 + 5)
                    dve.tensor_tensor(gel_y[:], gel_y[:], Y[:, 0:T], ALU.add).then_inc(gelu_step, 1)
                    dve.wait_ge(gelu_step, n * 5 + 6)
                    dve.scalar_tensor_tensor(out=gel_t[:], in0=gel_y[:], scalar=0.044715, in1=gel_y[:],
                                             op0=ALU.mult, op1=ALU.mult).then_inc(gelu_step, 1)
                    dve.wait_ge(gelu_step, n * 5 + 7)
                    dve.scalar_tensor_tensor(out=gel_t[:], in0=gel_t[:], scalar=1.0, in1=gel_y[:],
                                             op0=ALU.add, op1=ALU.mult).then_inc(gelu_step, 1)
                    dve.wait_ge(gelu_act, n * 2 + 1)
                    dve.scalar_tensor_tensor(out=gel_t[:], in0=gel_t[:], scalar=1.0, in1=gel_y[:],
                                             op0=ALU.add, op1=ALU.mult).then_inc(gelu_step, 1)
                    dve.wait_ge(gelu_act, n * 2 + 2)
                    dve.scalar_tensor_tensor(out=part_of(gT, turn, 1), in0=gel_t[:], scalar=0.5,
                                             in1=part_of(gT, turn, 0).bitcast(F32), op0=ALU.mult,
                                             op1=ALU.subtract).then_inc(gelu_step, 1)
                    if not last:
                        dve.wait_ge(bu_done, n * 4 + 4)
                        tile(9, u_f)
                    out_lo(2, VO, part_of(sbT, turn * 2 + 1, 1), part_of(sbT, turn * 2 + 1, 0))

                with dve.Fori(0, 3) as i:
                    branch_turn("BR", i, i)
                branch_turn("BL", 0, 3)
                for c in range(2):
                    split_next("GLU", l, 0, c)
                    for h in range(2):
                        t = 2 * c + h
                        if l + t > 0:
                            dve.wait_ge(glu_m, 4 * l + t)
                        for k in (2 * t, 2 * t + 1):
                            take("GLU", l, 0, k, bank[k % 4], gate[:, k % 2, :])
                        dve.wait_ge(glu_th, 4 * l + t + 1)
                        if l + t > 0:
                            dve.wait_ge(glu_lo, 4 * l + t)
                        dve.scalar_tensor_tensor(out=acc[:], in0=gate[:, 1, :], scalar=1.0, in1=gate[:, 0, :],
                                                 op0=ALU.add, op1=ALU.mult).then_inc(glu_m, 1)
                        dve.wait_ge(glu_hi, 4 * l + t + 1)
                        dve.scalar_tensor_tensor(out=ssmT[:, t, T:2 * T], in0=acc[:], scalar=0.5,
                                                 in1=ssmT[:, t, 0:T].bitcast(F32), op0=ALU.mult,
                                                 op1=ALU.subtract).then_inc(glu_lo, 1)
                dve.wait_ge(glu_lo, 4 * l + 4)
                with dve.Fori(0, 16) as i:
                    n = i + 16 * l
                    for b, c, k in GATES:
                        split_next("G", l, i, c)
                        if b == 0:
                            dve.wait_ge(merge_step, n * 5 + 5)
                        take("G", l, i, k, bank[k], gate[:, b, :])
                        if b == 0:
                            split_next("G", l, i, 1)
                            for k in range(3):
                                take("G", l, i, 1 + k, bank[1 + k], bran[:, k, :], 0.5)
                            dve.wait_ge(tile_out, tile_no("G", l, i, 3) + (1 + TILE_CREDIT))
                        dve.wait_ge(gate_th, n * 3 + (b + 1))
                        if b == 0:
                            dve.wait_ge(merge_lo, n + 1)
                            dve.scalar_tensor_tensor(out=acc[:], in0=gate[:, 0, :], scalar=1.0, in1=bran[:, 0, :],
                                                     op0=ALU.add, op1=ALU.mult).then_inc(merge_step, 1)
                        else:
                            dve.wait_ge(merge_step, n * 5 + (2 * b - 1 + 5))
                            dve.scalar_tensor_tensor(out=part[:], in0=gate[:, b, :], scalar=1.0,
                                                     in1=bran[:, b, :], op0=ALU.add, op1=ALU.mult
                                                     ).then_inc(merge_step, 1)
                            dve.wait_ge(merge_step, n * 5 + (2 * b + 5))
                            dve.tensor_tensor(acc[:], acc[:], part[:], ALU.add).then_inc(merge_step, 1)
                if l:
                    dve.wait_ge(resid_act, 4 * (2 * l - 1) + 4)
                    dve.wait_ge(resid_dve, 4 * (2 * l - 1) + 4)
                else:
                    dve.wait_ge(consts, 3)
                with dve.Fori(0, 2) as i:
                    for c in range(8):
                        split_next("WO", l, i, c)
                        if c % 4 == 3:
                            nn = c // 4
                            for m in range(TT):
                                add_rows("WO", l, i, nn, m, bank[6 - 2 * nn + m],
                                         stats=st[:, m, bass.ds(i * 2 + nn, 1), :],
                                         ready=chunk_no("WO", l, i, c) * 2 + (2 + HALF_CREDIT),
                                         dyn=i * 1024 + 512 * nn)
                norm(l, 0)
                last_l = l == DEPTH - 1

                def ffn_turn(i, last):
                    n = i + 11 * l
                    for c in range(12):
                        if last and c == 11:
                            if not last_l:
                                for h in range(2):
                                    lo_half(PHASES["U"][1][0], h, h, chunk_no("U", l + 1, 0, 0) * 2 + h)
                        else:
                            split_next("FF", l, i, c)
                        if c < 8:
                            f = c // 2
                            b = bank[2 * (f % 2) + c % 2]
                            if c % 2 == 0:
                                dve.wait_ge(ffn_step, n * 8 + (2 * f + 1))
                                take("FF", l, i, c, b, gg[:, f % 2, :])
                            else:
                                dve.wait_ge(ffn_step, n * 8 + (2 * f + 2))
                                take("FF", l, i, c, b, uu[:, f % 2, :])
                                dve.wait_ge(ffn_th, n * 4 + (f + 1))
                                dve.wait_ge(ffn_lo, n * 4 + (f + 1))
                                dve.scalar_tensor_tensor(out=hh[:, f % 2, :], in0=th[:, f % 2, :], scalar=1.0,
                                                         in1=gg[:, f % 2, :], op0=ALU.add, op1=ALU.mult
                                                         ).then_inc(ffn_step, 1)
                                dve.wait_ge(ffn_step, n * 8 + (2 * f + 1 + 4))
                                dve.wait_ge(tile_out, tile_no("FF", l, i, c) + (1 + TILE_CREDIT))
                                dve.scalar_tensor_tensor(out=hh[:, f % 2, :], in0=hh[:, f % 2, :], scalar=0.5,
                                                         in1=uu[:, f % 2, :], op0=ALU.mult, op1=ALU.mult
                                                         ).then_inc(ffn_step, 1)
                                dve.wait_ge(ffn_hi, n * 4 + (f + 1))
                                dve.tensor_tensor(mT[:, f, T:2 * T], hh[:, f % 2, :], mT[:, f, 0:T].bitcast(F32),
                                                  ALU.subtract).then_inc(ffn_lo, 1)
                        else:
                            nn = c - 8
                            if nn == 0:
                                dve.wait_ge(resid_act, 4 * (2 * l) + 4)
                                dve.wait_ge(resid_dve, 4 * (2 * l) + 4)
                                dve.wait_ge(rows_out, rows_no("FF", l, i, 0, 0) + ROWS_CREDIT)
                            for m in range(TT):
                                add_rows("FF", l, i, nn, m, bank[6 - 2 * (nn % 2) + m],
                                         stats=st[:, m, nn, :] if last else None,
                                         ready=chunk_no("FF", l, i, c) * 2 + (2 + HALF_CREDIT))

                with dve.Fori(0, 10) as i:
                    ffn_turn(i, False)
                ffn_turn(10, True)
                norm(l, 1)

        @block.tensor
        def _(pe):
            def product(ph, l, i, c, h, dst, x_t, k0, first, last):
                gh = chunk_no(ph, l, i, c) * 2 + h
                s = hl_slot(ph, c, h)
                pe.wait_ge(lo_ready, gh + (1 + HALF_CREDIT))
                for k in range(8):
                    w = slice(k * P, (k + 1) * P)
                    pe.matmul(dst[:, :], hi[:, s, w], x_t[:, k0 + k, :], start=first and k == 0, stop=False)
                    ins = pe.matmul(dst[:, 0:T], lo[:, s, w], x_t[:, k0 + k, 0:T], start=False,
                                    stop=last and k == 7)
                ins.then_inc(half_done, 1)

            def rows_product(ph, l, i, c, h, k0, banks, first, last, ready=None):
                gh = chunk_no(ph, l, i, c) * 2 + h
                s = hl_slot(ph, c, h)
                pe.wait_ge(lo_ready, gh + (1 + HALF_CREDIT))
                for m in range(TT):
                    for k in range(2):
                        if ready is not None:
                            pe.wait_ge(*ready(k0 + k))
                        xh = mT[:, k0 + k, m * P:(m + 1) * P]
                        xl = mT[:, k0 + k, T + m * P:T + (m + 1) * P]
                        wh, wl = hi[:, s, k * 512:(k + 1) * 512], lo[:, s, k * 512:(k + 1) * 512]
                        pe.matmul(banks[m][:, :], xh, wh, start=first and k == 0, stop=False)
                        pe.matmul(banks[m][:, :], xh, wl, start=False, stop=False)
                        ins = pe.matmul(banks[m][:, :], xl, wh, start=False, stop=last and k == 1)
                ins.then_inc(half_done, 1)

            pe.wait_ge(masks, 10)
            pe.wait_ge(ssm_in, 48)
            pe.wait_ge(setup, 2)
            for a in range(3):
                ins = pe.transpose(bank[1][:, 32 * a:32 * a + 32], ssm_nat[0:GROUPS, a, :], ident[0:GROUPS, 0:GROUPS])
            ins.then_inc(ssm_T, 1)
            for k in range(2 * KD):
                src = rows if k < KD else mem_rows
                if k == 0:
                    pe.wait_ge(x_in, 16)
                if k == KD:
                    pe.wait_ge(mem_in, 16)
                if k >= 4:
                    pe.wait_ge(init_lo, k - 3)
                for m in range(TT):
                    ins = pe.transpose(bank[4 + k % 4][:, m * P:(m + 1) * P],
                                       src[:, m, (k % KD) * P:(k % KD + 1) * P], ident[:])
                ins.then_inc(init_T, 1)
            pe.wait_ge(par_in, 16 * 12)
            for a, n in ((0, 116), (1, 116), (2, 64)):
                ins = pe.transpose(bank[0][:, a * P:a * P + n], par_nat[0:n, a, :], ident[0:n, 0:n])
            ins.then_inc(par_T, 1)
            pe.wait_ge(ssm_out, 1)
            pe.wait_ge(par_out, 2)
            pe.wait_ge(init_lo, 2 * KD)
            pe.wait_ge(consts, 2)

            def norm(l, which):
                v = 2 * l + which
                for k in range(KD):
                    pe.wait_ge(norm_done, 8 * v + 2 * (k // 4) + 2)
                    if k >= 4:
                        if k % 2:
                            pe.wait_ge(aff_act, 8 * v + (k - 4) // 2 + 1)
                        else:
                            pe.wait_ge(aff_dve, 8 * v + (k - 4) // 2 + 1)
                    for m in range(TT):
                        ins = pe.transpose(bank[4 + k % 4][:, m * P:(m + 1) * P], rows[:, m, k * P:(k + 1) * P],
                                           ident[:])
                    ins.then_inc(ln_T, 1)
                for n in range(4):
                    if n == 0:
                        ph = "FF" if which else "G"
                        pe.wait_ge(tile_out, tile_no(ph, l, PHASES[ph][0] - 1, TILES[ph] - 1) + 1 + TILE_CREDIT)
                    pe.wait_ge(xs_lo, 16 * v + (4 * n + 4 if n < 2 else 16))
                    for m in range(TT):
                        for k in range(4):
                            o = bank[2 * n + m][:, k * P:(k + 1) * P]
                            kk = 4 * n + k
                            pe.matmul(o, xs[:, kk, m * P:(m + 1) * P], ident_r[:], start=True, stop=False)
                            ins = pe.matmul(o, xs[:, kk, T + m * P:T + (m + 1) * P], ident_r[:], start=False,
                                            stop=True)
                        ins.then_inc(rebuilt, 1)

            for l in range(DEPTH):
                if l:
                    pe.wait_ge(resid_act, 4 * (2 * l - 1) + 4)
                    pe.wait_ge(resid_dve, 4 * (2 * l - 1) + 4)
                if l:
                    pe.wait_ge(memT_full, 16 * l)
                for c, x_t in ((0, mT), (1, xs)):
                    pe.wait_ge(tile_out, tile_no("U", l, 0, c) + 1)
                    for h in range(2):
                        product("U", l, 0, c, h, bank[c], x_t, 8 * h, h == 0, h == 1)

                if l == 0:
                    pe.wait_ge(setup, BLOCK_STEPS)
                    pe.wait_ge(c_out, 4)
                    for q in range(8):
                        if q >= 2:
                            pe.wait_ge(tab_out, q - 1)
                        for r in range(4):
                            src = (b_blk, c_blk)[r // 2][:, r % 2, q, :]
                            ins = pe.transpose(bank[2 + q % 2][:, r * P:(r + 1) * P], src, ident[:])
                        ins.then_inc(tab_T, 1)
                    pe.wait_ge(tab_out, 8)

                def branch_turn(ph, i, turn):
                    n = turn + 4 * l
                    last = ph == "BL"

                    def half(c, x_t, h):
                        if h == 0:
                            pe.wait_ge(tile_out, tile_no(ph, l, i, c) + 1)
                        product(ph, l, i, c, h, bank[c % 2], x_t, 8 * h, h == 0, h == 1)

                    def gemm(c, x_t):
                        half(c, x_t, 0)
                        half(c, x_t, 1)

                    def got(c):
                        pe.wait_ge(tile_out, tile_no(ph, l, i, c) + (1 + TILE_CREDIT))

                    def bu(j):
                        pe.wait_ge(bu_copied, n * 4 + (j + 1))
                        r = slice(32 * j, 32 * j + 32)
                        for a in range(2):
                            ins = pe.matmul(BU[j % 2][:, a * T:(a + 1) * T], tab[r, a, :], u_f[r, :],
                                            start=True, stop=True, tile_position=(32 * j, 0))
                        ins.then_inc(bu_done, 1)

                    def y_part(j):
                        pe.wait_ge(ks_step, n * (12 * SCAN_STEPS) + (6 * SCAN_STEPS * (j // 2 + 1) + 1))
                        if j == 0:
                            pe.wait_ge(gelu_step, n * 5 + 1)
                        r = slice(32 * j, 32 * j + 32)
                        for a in range(2):
                            ins = pe.matmul(Y[r, 0:T], tab[:, 2 + a, r], scan[:, j, a, :],
                                            start=a == 0, stop=a == 1, tile_position=(0, 32 * j))
                        ins.then_inc(y_done, 1)

                    def z(e):
                        pe.wait_ge(w_ready, n * 2 + (e + 1))
                        pe.matmul(Z[:, 0:T], k_f[:, 0:P], q_f[:], start=True, stop=False, skip_group_check=True)
                        pe.matmul(Z[:, T:384], k_f[:, P:T], q_f[:, P:T], start=False, stop=False,
                                  skip_group_check=True).then_inc(z_done, 1)

                    def tri(e):
                        pe.wait_ge(sp_step, n * 4 + (2 * e + 4))
                        pe.matmul(Z[:, 0:T], ntri[:], sp_t[:, 0:T], start=False, stop=False, skip_group_check=True)
                        pe.matmul(Z[:, P:T], nones[:], sp_t[:, T:384], start=False, stop=False,
                                  skip_group_check=True)
                        pe.matmul(Z[:, T:384], ntri[:], sp_t[:, T:384], start=False, stop=False,
                                  skip_group_check=True)
                        pe.matmul(Z[:, 0:P], ident_b[:], nbig[:], start=False, stop=False, skip_group_check=True)
                        pe.matmul(Z[:, T:384], ident_b[:], nbig[:], start=False, stop=True,
                                  skip_group_check=True).then_inc(tri_done, 1)

                    def v_turn(k, src, o):
                        pe.wait_ge(v_copied, n * 3 + (k + 1))
                        for t in range(2):
                            ins = pe.transpose(o[:, t * P:(t + 1) * P], src[:, t * P:(t + 1) * P], ident[:])
                        ins.then_inc(vt_done, 1)

                    def attend(e):
                        pe.wait_ge(w_ready, n * 2 + (e + 2))
                        pe.wait_ge(v_copied, n * 3 + (2 + 2 * e))
                        pe.wait_ge(o_lo, n * 3 + (e + 1))
                        pe.matmul(VO[:, T:2 * T], v_s[:, 0, :], w_t[:, 0:T], start=True, stop=False)
                        pe.matmul(VO[:, T + P:2 * T], v_s[:, 1, :], w_t[:, T:384], start=False, stop=True
                                  ).then_inc(attn_done, 1)

                    half(0, xs, 0)
                    pe.wait_ge(tab_b_full, n * 16 + 16)
                    got(-1)
                    bu(0)
                    bu(1)
                    half(0, xs, 1)
                    half(1, mT, 0)
                    bu(2)
                    bu(3)
                    half(1, mT, 1)
                    gemm(2, xs)
                    got(1)
                    pe.wait_ge(pt_copied, n + 1)
                    pe.wait_ge(o_lo, n * 3 + 1)
                    for t in range(TT):
                        ins = pe.matmul(S[:, t * T:(t + 1) * T], qm_f[:, t * P:(t + 1) * P], km_f[:], start=True,
                                        stop=True)
                    ins.then_inc(s_done, 1)
                    gemm(3, xs)
                    gemm(4, xs)
                    got(3)
                    z(0)
                    pe.wait_ge(sm_step, n * 5 + 10)
                    for mt in range(2):
                        for t in range(TT):
                            ins = pe.transpose(S[:, mt * T + t * P:mt * T + (t + 1) * P],
                                               prob[:, t, mt * P:(mt + 1) * P], ident[:])
                    ins.then_inc(pt_done, 1)
                    gemm(5, xs)
                    got(4)
                    v_turn(0, v_f, VO)
                    tri(0)
                    pe.wait_ge(tab_c_full, n * 16 + 16)
                    y_part(0)
                    y_part(1)
                    gemm(6, xs)
                    attend(0)
                    pe.wait_ge(pt_copied, n + 2)
                    v_turn(1, vm_f, S)
                    gemm(7, xs)
                    pe.wait_ge(v_copied, n * 3 + 3)
                    for mt in range(2):
                        ins = pe.matmul(S[:, T:2 * T], vm_s[:, mt, :], probT[:, mt, :], start=mt == 0, stop=mt == 1)
                    ins.then_inc(attn_done, 1)
                    got(6)
                    z(1)
                    if not last:
                        gemm(8, mT)
                    got(7)
                    pe.wait_ge(o_lo, n * 3 + 2)
                    v_turn(2, v_f, VO)
                    tri(1)
                    if not last:
                        half(9, xs, 0)
                    y_part(2)
                    y_part(3)
                    if not last:
                        half(9, xs, 1)
                    attend(1)

                with pe.Fori(0, 3) as i:
                    branch_turn("BR", i, i)
                branch_turn("BL", 0, 3)
                pe.wait_ge(gelu_step, (4 * l + 3) * 5 + 10)
                pe.wait_ge(bu_copied, 16 * l + 18)
                for c in range(2):
                    for h in range(2):
                        t = 2 * c + h
                        s = hl_slot("GLU", c, h)
                        pe.wait_ge(lo_ready, chunk_no("GLU", l, 0, c) * 2 + h + 1 + HALF_CREDIT)
                        for ab in range(2):
                            kk = 2 * t + ab
                            pe.wait_ge(tile_out, tile_no("GLU", l, 0, kk) + 1)
                            dst = bank[kk % 4]
                            for k in range(4):
                                w = slice(k * 256 + ab * P, k * 256 + (ab + 1) * P)
                                pe.matmul(dst[:, :], hi[:, s, w], gT[:, k, :], start=k == 0, stop=False)
                                ins = pe.matmul(dst[:, 0:T], lo[:, s, w], gT[:, k, 0:T], start=False, stop=k == 3)
                        ins.then_inc(half_done, 1)
                pe.wait_ge(w_ready, 8 * (l + 1) + 1)
                pe.wait_ge(pt_copied, 4 * (l + 1) + 1)
                pe.wait_ge(o_lo, 12 * (l + 1) + 1)
                with pe.Fori(0, 16) as i:
                    def gate_product(c, k):
                        pe.wait_ge(tile_out, tile_no("G", l, i, k) - 1)
                        for h in range(2):
                            product("G", l, i, c, h, bank[k], xs, 8 * h, h == 0, h == 1)

                    gate_product(0, 0)
                    pe.wait_ge(tile_out, tile_no("G", l, i, 1) - 1)
                    product("G", l, i, 1, 0, bank[1], sbT, 0, True, True)
                    pe.wait_ge(glu_lo, 4 * l + 4)
                    pe.wait_ge(lo_ready, chunk_no("G", l, i, 1) * 2 + (2 + HALF_CREDIT))
                    s = hl_slot("G", 1, 1)
                    for b, src in ((1, ssmT), (2, mmT)):
                        pe.wait_ge(tile_out, tile_no("G", l, i, 1 + b) - 1)
                        for k in range(4):
                            w = slice((4 * (b - 1) + k) * P, (4 * (b - 1) + k + 1) * P)
                            pe.matmul(bank[1 + b][:, :], hi[:, s, w], src[:, k, :], start=k == 0, stop=False)
                            ins = pe.matmul(bank[1 + b][:, 0:T], lo[:, s, w], src[:, k, 0:T], start=False, stop=k == 3)
                    ins.then_inc(half_done, 1)
                    gate_product(2, 4)
                    gate_product(3, 5)
                pe.wait_ge(tile_out, tile_no("G", l, 15, 5) + 1 + TILE_CREDIT)
                pe.wait_ge(merge_lo, 16 * l + 17)
                with pe.Fori(0, 2) as i:
                    for nn in range(2):
                        for m in range(TT):
                            pe.wait_ge(rows_out, rows_no("WO", l, i, nn, m) + 1)
                        banks = [bank[6 - 2 * nn + m] for m in range(TT)]
                        for c in range(4):
                            for h in range(2):
                                rows_product("WO", l, i, 4 * nn + c, h, 4 * c + 2 * h, banks, c == 0 and h == 0,
                                             c == 3 and h == 1)
                norm(l, 0)
                pe.wait_ge(resid_act, 4 * (2 * l) + 2)
                pe.wait_ge(resid_dve, 4 * (2 * l) + 2)
                with pe.Fori(0, 11) as i:
                    n = i + 11 * l
                    for c in range(8):
                        pe.wait_ge(tile_out, tile_no("FF", l, i, c) - 1)
                        for h in range(2):
                            product("FF", l, i, c, h, bank[2 * ((c // 2) % 2) + c % 2], xs, 8 * h, h == 0, h == 1)
                    pe.wait_ge(resid_act, 4 * (2 * l) + 4)
                    pe.wait_ge(resid_dve, 4 * (2 * l) + 4)
                    for nn in range(4):
                        for m in range(TT):
                            pe.wait_ge(rows_out, rows_no("FF", l, i, nn, m) + 1)
                        banks = [bank[6 - 2 * (nn % 2) + m] for m in range(TT)]
                        for h in range(2):
                            rows_product("FF", l, i, 8 + nn, h, 2 * h, banks, h == 0, h == 1,
                                         ready=(lambda k: (ffn_lo, n * 4 + (k + 3))) if nn == 0 else None)
                if l < DEPTH - 1:
                    norm(l, 1)


def hl_slot(ph, c, h):
    return (2 * c + h) % HLS


ANGLE_STEPS = 25
DT_STEPS = 39
BLOCK_STEPS = 62
SETUP_STEPS = 107

_INS = ["x", "mem", "w_in", "b_in", "sb_w_out", "ssm_lambda_re", "ssm_lambda_im", "ssm_log_dt", "ssm_b_re",
        "ssm_b_im", "ssm_c_re", "ssm_c_im", "ssm_d", "ssm_w_glu", "ssm_w_out", "mem_w_kv", "mem_w_out", "w_o",
        "ln1_g", "ln1_b", "ffn_w_gate_up", "ffn_w_down", "ln2_g", "ln2_b"]


def kernel(**inputs):
    import concourse.bacc as bacc
    from concourse.bass_utils import run_bass_kernel_spmd

    nc = bacc.Bacc("TRN2", target_bir_lowering=False, num_devices=1, dynamic_dma_scratch_size=1024)
    arrays, args = {}, []
    for name in _INS:
        a = np.ascontiguousarray(inputs[name])
        arrays[f"in_{name}"] = a
        args.append(nc.dram_tensor(f"in_{name}", a.shape, mybir.dt.from_np(a.dtype), kind="ExternalInput").ap())
    out = nc.dram_tensor("out_x", (1, T, D), F32, kind="ExternalOutput").ap()
    trunk(nc, *args, out)
    r = run_bass_kernel_spmd(nc, [arrays], core_ids=[0])
    return r.results[0]["out_x"]
```
